# Optimizing a Trainium2 kernel written in Bass

```python
import math
import jax
import jax.numpy as jnp
from jax import lax
import numpy as np

D_MODEL = 1024
BATCH = 1
SEQ = 128
DEPTH = 2
DEC_BATCH = 1
DEC_SEQ = 256
PAST_LEN = 128

GRID_W = 64
N_MIXERS = 2
N_LAYERS_A = (DEPTH + 1) // 2
N_LAYERS_B = DEPTH // 2
HD_A = 64
H_A = D_MODEL // (2 * HD_A)
H_B = 16
HD_B = D_MODEL // H_B
NA_KH = 8
NA_KW = 16
ROPE_BASE = 10000.0
N_GROUPS = 4
EXP_PER_GROUP = 8
N_EXPERTS = N_GROUPS * EXP_PER_GROUP
TOP_K = 2
D_EXPERT = 512
MOE_BLOCK = 128
Q_BLOCK = 128
LN_EPS = 1e-5
DEEPNORM_ALPHA = (2.0 * DEPTH) ** 0.25
DEEPNORM_BETA = (8.0 * DEPTH) ** -0.25

kernel_name = 'hybrid_diffattn_natten_hmoe_prefix_step'

def layer_norm(x, g, b):
    xf = x.astype(jnp.float32)
    mu = jnp.mean(xf, -1, keepdims=True)
    var = jnp.mean(jnp.square(xf - mu), -1, keepdims=True)
    y = (xf - mu) * lax.rsqrt(var + LN_EPS)
    return (y * g.astype(jnp.float32) + b.astype(jnp.float32)).astype(x.dtype)

def rms_norm(x, g):
    xf = x.astype(jnp.float32)
    y = xf * lax.rsqrt(jnp.mean(jnp.square(xf), -1, keepdims=True) + LN_EPS)
    return (y * g.astype(jnp.float32)).astype(x.dtype)

def adaln(cond, w_ada_i, b_ada_i):
    m = jax.nn.silu(cond) @ w_ada_i + b_ada_i
    return jnp.split(m[..., None, :], 6, axis=-1)

def mod_in(x, shift, scale):
    return x * (1 + scale) + shift

def axial_rope_tables(n_tok, dim):
    t = jnp.arange(n_tok)
    pos = jnp.stack([t // GRID_W, t % GRID_W], -1).astype(jnp.float32)
    quarter = dim // 4
    inv_freq = ROPE_BASE ** (-jnp.arange(quarter, dtype=jnp.float32) / quarter)
    ang = pos[:, :, None] * inv_freq
    return jnp.cos(ang), jnp.sin(ang)

def apply_axial_rope(x, cos, sin):
    B, T, H, dim = x.shape
    xa = x.reshape(B, T, H, 2, 2, dim // 4).astype(jnp.float32)
    x1, x2 = xa[..., 0, :], xa[..., 1, :]
    cs, sn = cos[None, :, None], sin[None, :, None]
    out = jnp.stack([x1 * cs - x2 * sn, x2 * cs + x1 * sn], axis=-2)
    return out.reshape(B, T, H, dim).astype(x.dtype)

def diff_qkv(h, w_qkv):
    B, T, _ = h.shape
    q, k, v = jnp.split(h @ w_qkv, 3, -1)
    return (q.reshape(B, T, 2 * H_A, HD_A), k.reshape(B, T, 2 * H_A, HD_A),
            v.reshape(B, T, H_A, 2 * HD_A))

def diff_lambda_init(layer_idx):
    return 0.8 - 0.6 * math.exp(-0.3 * layer_idx)

def diff_lambda(lam_p, lam_init):
    lp = lam_p.astype(jnp.float32)
    return jnp.exp(jnp.sum(lp[0] * lp[1])) - jnp.exp(jnp.sum(lp[2] * lp[3])) + lam_init

def diff_attention(q, k, v, lam):
    B, Tq = q.shape[:2]
    nb = Tq // Q_BLOCK
    scale = HD_A ** -0.5
    qb = jnp.moveaxis(q.reshape(B, nb, Q_BLOCK, 2 * H_A, HD_A), 1, 0)

    def one_block(qi):
        s = jnp.einsum('bqhd,bkhd->bhqk', qi, k).astype(jnp.float32) * scale
        p = jax.nn.softmax(s, -1).reshape(B, H_A, 2, Q_BLOCK, -1)
        a = p[:, :, 0] - lam * p[:, :, 1]
        return jnp.einsum('bhqk,bkhe->bqhe', a.astype(v.dtype), v)

    o = lax.map(one_block, qb)
    return jnp.moveaxis(o, 0, 1).reshape(B, Tq, H_A, 2 * HD_A)

def diff_output(o, lam_init, subln_g, w_o):
    B, T = o.shape[:2]
    o = rms_norm(o, subln_g) * (1.0 - lam_init)
    return o.reshape(B, T, D_MODEL) @ w_o

def na_qkv(h, w_qkv):
    B, T, _ = h.shape
    q, k, v = jnp.split(h @ w_qkv, 3, -1)
    return q.reshape(B, T, H_B, HD_B), k.reshape(B, T, H_B, HD_B), v.reshape(B, T, H_B, HD_B)

def dense_attention(q, k, v):
    B, T, H, d = q.shape
    nb = T // Q_BLOCK
    qb = jnp.moveaxis(q.reshape(B, nb, Q_BLOCK, H, d), 1, 0)

    def one_block(qi):
        s = jnp.einsum('bqhd,bkhd->bhqk', qi, k).astype(jnp.float32) * (d ** -0.5)
        p = jax.nn.softmax(s, -1).astype(v.dtype)
        return jnp.einsum('bhqk,bkhd->bqhd', p, v)

    o = lax.map(one_block, qb)
    return jnp.moveaxis(o, 0, 1).reshape(B, T, H, d)

def neighborhood_attention(q, k, v, k_ctx, v_ctx, rpb):
    B, S, H, d = q.shape
    rows = S // GRID_W
    kh = min(NA_KH, rows)
    kw = NA_KW
    scale = d ** -0.5
    qg = q.reshape(B, rows, GRID_W, H, d)
    kg = k.reshape(B, rows, GRID_W, H, d)
    vg = v.reshape(B, rows, GRID_W, H, d)
    col = np.arange(GRID_W)
    col_start = np.clip(col - kw // 2, 0, GRID_W - kw)
    col_idx = col_start[:, None] + np.arange(kw)[None, :]
    col_off = col_idx - col[:, None] + (NA_KW - 1)
    rpb_cols = rpb[:, :, col_off]

    def one_row(r):
        r_start = jnp.clip(r - kh // 2, 0, rows - kh)
        q_r = lax.dynamic_index_in_dim(qg, r, axis=1, keepdims=False)
        k_band = lax.dynamic_slice_in_dim(kg, r_start, kh, axis=1)
        v_band = lax.dynamic_slice_in_dim(vg, r_start, kh, axis=1)
        k_nb = k_band[:, :, col_idx]
        v_nb = v_band[:, :, col_idx]
        row_off = r_start + jnp.arange(kh) - r + (NA_KH - 1)
        bias = jnp.transpose(jnp.take(rpb_cols, row_off, axis=1), (0, 2, 1, 3))
        s_nb = jnp.einsum('bqhd,biqjhd->bhqij', q_r, k_nb).astype(jnp.float32) * scale
        s_nb = s_nb + bias[None].astype(jnp.float32)
        s_ctx = jnp.einsum('bqhd,bphd->bhqp', q_r, k_ctx).astype(jnp.float32) * scale
        s = jnp.concatenate([s_nb.reshape(B, H, GRID_W, kh * kw), s_ctx], -1)
        p = jax.nn.softmax(s, -1).astype(v.dtype)
        p_nb = p[..., :kh * kw].reshape(B, H, GRID_W, kh, kw)
        p_ctx = p[..., kh * kw:]
        return (jnp.einsum('bhqij,biqjhd->bqhd', p_nb, v_nb)
                + jnp.einsum('bhqp,bphd->bqhd', p_ctx, v_ctx))

    o = lax.map(one_row, jnp.arange(rows))
    return jnp.moveaxis(o, 0, 1).reshape(B, S, H, d)

def hier_moe(h, w_rg, b_rg, w_re, b_re, w_gate, w_up, w_down):
    B, T, D = h.shape
    xt = h.reshape(B * T, D)
    n = xt.shape[0]
    g_logits = (xt @ w_rg).astype(jnp.float32) + b_rg.astype(jnp.float32)
    g_sel = jnp.argmax(g_logits, -1)
    p_g = jnp.take_along_axis(jax.nn.softmax(g_logits, -1), g_sel[:, None], -1)
    e_logits = ((xt @ w_re).astype(jnp.float32) + b_re.astype(jnp.float32)).reshape(n, N_GROUPS, EXP_PER_GROUP)
    e_in_group = jnp.take_along_axis(e_logits, g_sel[:, None, None], 1)[:, 0]
    top_v, top_i = lax.top_k(e_in_group, TOP_K)
    gates = jax.nn.softmax(top_v, -1) * p_g
    experts = g_sel[:, None] * EXP_PER_GROUP + top_i
    flat_e = experts.reshape(-1)
    flat_t = jnp.repeat(jnp.arange(n, dtype=jnp.int32), TOP_K)
    flat_w = gates.reshape(-1)
    order = jnp.argsort(flat_e)
    se, st, sw = flat_e[order], flat_t[order], flat_w[order]
    counts = jnp.bincount(flat_e, length=N_EXPERTS)
    starts = jnp.cumsum(counts) - counts
    padded = (counts + MOE_BLOCK - 1) // MOE_BLOCK * MOE_BLOCK
    pend = jnp.cumsum(padded)
    pstart = pend - padded
    dest = pstart[se] + (jnp.arange(n * TOP_K) - starts[se])
    n_blocks = -(-(n * TOP_K + N_EXPERTS * (MOE_BLOCK - 1)) // MOE_BLOCK)
    tok_buf = jnp.zeros(n_blocks * MOE_BLOCK, jnp.int32).at[dest].set(st)
    w_buf = jnp.zeros(n_blocks * MOE_BLOCK, jnp.float32).at[dest].set(sw)
    blk_e = jnp.minimum(jnp.searchsorted(pend, jnp.arange(n_blocks) * MOE_BLOCK, side='right'), N_EXPERTS - 1)

    def one_block(args):
        tok, e, w = args
        xb = xt[tok]
        hb = jax.nn.silu(xb @ w_gate[e]) * (xb @ w_up[e])
        return (hb @ w_down[e]) * w[:, None].astype(h.dtype)

    out = lax.map(one_block, (tok_buf.reshape(n_blocks, MOE_BLOCK), blk_e, w_buf.reshape(n_blocks, MOE_BLOCK)))
    y = jnp.zeros_like(xt).at[tok_buf].add(out.reshape(-1, D))
    return y.reshape(B, T, D)

def setup_inputs(seed: int = 0) -> dict:
    key = jax.random.key(seed)
    ks = jax.random.split(key, 26)
    f32 = jnp.float32
    D = D_MODEL

    def nrm(k, shape, scale):
        return jax.random.normal(k, shape, f32) * scale

    return {
        'x_prompt': nrm(ks[0], (BATCH, SEQ, D), 1.0),
        'x_sample': nrm(ks[1], (DEC_BATCH, DEC_SEQ, D), 1.0),
        'cache_a_k': nrm(ks[2], (DEC_BATCH, N_LAYERS_A, PAST_LEN, 2 * H_A, HD_A), 1.0),
        'cache_a_v': nrm(ks[3], (DEC_BATCH, N_LAYERS_A, PAST_LEN, H_A, 2 * HD_A), 1.0),
        'cache_b_k': nrm(ks[4], (DEC_BATCH, N_LAYERS_B, PAST_LEN, H_B, HD_B), 1.0),
        'cache_b_v': nrm(ks[5], (DEC_BATCH, N_LAYERS_B, PAST_LEN, H_B, HD_B), 1.0),
        'c': nrm(ks[6], (DEC_BATCH, D), 1.0),
        'c_ctx': nrm(ks[7], (D,), 1.0),
        'w_ada': nrm(ks[8], (DEPTH, D, 6 * D), 0.5 * D ** -0.5),
        'b_ada': nrm(ks[9], (DEPTH, 6 * D), 0.02),
        'ln_g': 1.0 + nrm(ks[10], (DEPTH, 2, D), 0.02),
        'ln_b': nrm(ks[11], (DEPTH, 2, D), 0.02),
        'w_qkv_a': nrm(ks[12], (N_LAYERS_A, D, 3 * D), D ** -0.5),
        'lam_a': nrm(ks[13], (N_LAYERS_A, 4, HD_A), 0.1),
        'subln_a': 1.0 + nrm(ks[14], (N_LAYERS_A, 2 * HD_A), 0.02),
        'w_o_a': nrm(ks[15], (N_LAYERS_A, D, D), DEEPNORM_BETA * D ** -0.5),
        'w_qkv_b': nrm(ks[16], (N_LAYERS_B, D, 3 * D), D ** -0.5),
        'rpb_b': nrm(ks[17], (N_LAYERS_B, H_B, 2 * NA_KH - 1, 2 * NA_KW - 1), 0.02),
        'w_o_b': nrm(ks[18], (N_LAYERS_B, D, D), DEEPNORM_BETA * D ** -0.5),
        'w_rg': nrm(ks[19], (DEPTH, D, N_GROUPS), D ** -0.5),
        'b_rg': nrm(ks[20], (DEPTH, N_GROUPS), 0.01),
        'w_re': nrm(ks[21], (DEPTH, D, N_EXPERTS), D ** -0.5),
        'b_re': nrm(ks[22], (DEPTH, N_EXPERTS), 0.01),
        'w_gate': nrm(ks[23], (DEPTH, N_EXPERTS, D, D_EXPERT), D ** -0.5),
        'w_up': nrm(ks[24], (DEPTH, N_EXPERTS, D, D_EXPERT), D ** -0.5),
        'w_down': nrm(ks[25], (DEPTH, N_EXPERTS, D_EXPERT, D), DEEPNORM_BETA * D_EXPERT ** -0.5),
    }

def reference(x_prompt, x_sample, cache_a_k, cache_a_v, cache_b_k, cache_b_v, c, c_ctx,
              w_ada, b_ada, ln_g, ln_b, w_qkv_a, lam_a, subln_a, w_o_a, w_qkv_b, rpb_b, w_o_b,
              w_rg, b_rg, w_re, b_re, w_gate, w_up, w_down):

    def post_norm(i, slot, x, gate, out):
        return layer_norm(DEEPNORM_ALPHA * x + gate * out, ln_g[i, slot], ln_b[i, slot])

    def channel_mixer(i, x, sh, sc, g):
        out = hier_moe(mod_in(x, sh, sc), w_rg[i], b_rg[i], w_re[i], b_re[i],
                       w_gate[i], w_up[i], w_down[i])
        return post_norm(i, 1, x, g, out)

    x = x_prompt
    new_a_k, new_a_v, new_b_k, new_b_v = [], [], [], []
    for i in range(DEPTH):
        sh1, sc1, g1, sh2, sc2, g2 = adaln(c_ctx, w_ada[i], b_ada[i])
        h = mod_in(x, sh1, sc1)
        j = i // N_MIXERS
        if i % N_MIXERS == 0:
            q, k, v = diff_qkv(h, w_qkv_a[j])
            lam_init = diff_lambda_init(i)
            o = diff_attention(q, k, v, diff_lambda(lam_a[j], lam_init))
            out = diff_output(o, lam_init, subln_a[j], w_o_a[j])
            new_a_k.append(k)
            new_a_v.append(v)
        else:
            q, k, v = na_qkv(h, w_qkv_b[j])
            out = dense_attention(q, k, v).reshape(h.shape) @ w_o_b[j]
            new_b_k.append(k)
            new_b_v.append(v)
        x = post_norm(i, 0, x, g1, out)
        x = channel_mixer(i, x, sh2, sc2, g2)
    y_prompt = x

    x = x_sample
    n_lat = x.shape[1]
    cos, sin = axial_rope_tables(n_lat, HD_A)
    for i in range(DEPTH):
        sh1, sc1, g1, sh2, sc2, g2 = adaln(c, w_ada[i], b_ada[i])
        h = mod_in(x, sh1, sc1)
        j = i // N_MIXERS
        if i % N_MIXERS == 0:
            q, k, v = diff_qkv(h, w_qkv_a[j])
            q = apply_axial_rope(q, cos, sin)
            k = apply_axial_rope(k, cos, sin)
            k_all = jnp.concatenate([cache_a_k[:, j].astype(k.dtype), k], axis=1)
            v_all = jnp.concatenate([cache_a_v[:, j].astype(v.dtype), v], axis=1)
            lam_init = diff_lambda_init(i)
            o = diff_attention(q, k_all, v_all, diff_lambda(lam_a[j], lam_init))
            out = diff_output(o, lam_init, subln_a[j], w_o_a[j])
        else:
            q, k, v = na_qkv(h, w_qkv_b[j])
            o = neighborhood_attention(q, k, v, cache_b_k[:, j].astype(k.dtype),
                                       cache_b_v[:, j].astype(v.dtype), rpb_b[j])
            out = o.reshape(h.shape) @ w_o_b[j]
        x = post_norm(i, 0, x, g1, out)
        x = channel_mixer(i, x, sh2, sc2, g2)
    y_sample = x

    return (y_prompt, y_sample, jnp.stack(new_a_k, axis=1), jnp.stack(new_a_v, axis=1),
            jnp.stack(new_b_k, axis=1), jnp.stack(new_b_v, axis=1))


_drawn_inputs = setup_inputs


def setup_inputs(seed=0):
    import zlib

    import numpy as np

    out = dict(_drawn_inputs(seed))
    spreads = {}
    factors = {'cache_b_k': 6.238,
     'cache_b_v': 5.197,
     'lam_a': 8.0,
     'subln_a': 31.501,
     'rpb_b': 200.0,
     'b_rg': 54.463,
     'b_re': 64.0}
    for name, (base, spread) in spreads.items():
        noise = np.random.default_rng([zlib.crc32(name.encode()), seed]).standard_normal(out[name].shape)
        drawn = base * np.exp(spread * noise) if base else spread * noise
        out[name] = jnp.asarray(drawn.astype(out[name].dtype))
    for name, factor in factors.items():
        out[name] = (out[name] * factor).astype(out[name].dtype)
    return out
```

```python
from contextlib import ExitStack
import math

import numpy as np
import concourse.bass as bass
from concourse import mybir

P = 128
D = 1024
KD = D // P
NT = 3
LAYERS = 2
HEADS = 16
HD = 64
PAIRS = HEADS // 2
NE = 32
NG = 4
EPG = NE // NG
DE = 512
TOPK = 2
BLK = 64
NB = (NT * P * TOPK + NE * (BLK - 1)) // BLK
NBX = NB + 2
RING = 6
GU, DN = 4, 2
POOL_CHUNKS = (3, 5)
CH = 2048
GRID_W = 64
NA_KH, NA_KW = 8, 16
ROWS = 256 // GRID_W
BM = 6
SCALE = HD ** -0.5
ALPHA = (2.0 * LAYERS) ** 0.25
EPS = 1e-5
LAM_INIT = 0.8 - 0.6 * math.exp(0.0)
WO_K = (2, 2, 1, 1, 1, 1)
BIG = 1e30

F32 = mybir.dt.float32
F32R = mybir.dt.float32r
I32 = mybir.dt.int32
ACT = mybir.ActivationFunctionType
ALU = mybir.AluOpType
AX = mybir.AxisListType.X

C_ID, C_II, C_FLIP, C_TRI, C_ONE, C_IOTA, C_TOK, C_ROPE, C_WIN, C_ZERO, C_THR = np.cumsum(
    [0, P, BLK, P, P, P, P, NT, 2 * 2 * 32, GRID_W, P]).tolist()
C_N = C_THR + 8
T_LIST, T_ORD, T_FIRST, T_NACT, T_NBLK = 0, 32, 32 + 48, 32 + 96, 32 + 97
T_LAST = T_NBLK + 1
T_N = T_LAST + 1


def constants():
    c = np.zeros((P, C_N), np.float32)
    p = np.arange(P)
    c[p, C_ID + p] = 1.0
    c[p, C_II + p % BLK] = 1.0
    c[p, C_FLIP + (p // 64) * 64 + 63 - p % 64] = 1.0
    c[:, C_TRI:C_TRI + P] = p[:, None] < p[None, :]
    c[:, C_ONE:C_ONE + P] = 1.0
    c[:, C_IOTA:C_IOTA + P] = p[None, :]
    c[:, C_TOK:C_TOK + NT] = p[:, None] + P * np.arange(NT)[None, :]
    t = np.arange(256)
    pos = np.stack([t // GRID_W, t % GRID_W], -1).astype(np.float32)
    quarter = HD // 4
    inv = (np.float32(10000.0) ** (-np.arange(quarter, dtype=np.float32) / np.float32(quarter))).astype(np.float32)
    ang = (pos[:, :, None] * inv).reshape(2, P, 32)
    for i in range(2):
        c[:, C_ROPE + i * 64:C_ROPE + i * 64 + 32] = np.cos(ang[i])
        c[:, C_ROPE + i * 64 + 32:C_ROPE + i * 64 + 64] = np.sin(ang[i])
    q, k = p[:, None] % 64, np.arange(GRID_W)[None, :]
    start = np.clip(q - NA_KW // 2, 0, GRID_W - NA_KW)
    c[:, C_WIN:C_WIN + GRID_W] = np.where((k >= start) & (k < start + NA_KW), 0.0, -BIG)
    c[:, C_THR:C_THR + 6] = BLK * np.arange(6)[None, :]
    return c


def backbone_kernel(nc, x_prompt, x_sample, cache_a_k, cache_a_v, cache_b_k, cache_b_v, c, c_ctx,
                    w_ada, b_ada, ln_g, ln_b, w_qkv_a, lam_a, subln_a, w_o_a, w_qkv_b, rpb_b, w_o_b,
                    w_rg, b_rg, w_re, b_re, w_gate, w_up, w_down, consts,
                    y_prompt, y_sample, new_a_k, new_a_v, new_b_k, new_b_v):
    ctx = ExitStack()
    with ctx:
        def sb(name, shape, dt=F32):
            return ctx.enter_context(nc.sbuf_tensor(name, shape, dt))

        def overlay(tensors):
            with ExitStack() as s:
                return [s.enter_context(nc.sbuf_tensor(n, shape, dt)) for n, shape, dt in tensors]

        def sem(name):
            return ctx.enter_context(nc.semaphore(name))

        def sem2(name):
            return [sem(f"{name}_{l}") for l in range(LAYERS)]

        cst = sb("cst", [P, C_N])
        x = sb("x", [P, NT, D])
        raw = sb("raw", [P, RING, CH])
        modb = sb("modb", [P, 4, D])
        wr = sb("wr", [P, LAYERS, KD, NG + NE])
        br = sb("br", [P, LAYERS, NG + NE])
        condr = sb("condr", [P, 2, KD])
        cond = sb("cond", [P, KD, 2])
        lamb = sb("lamb", [P, 4 * HD])
        lam = sb("lam", [P, 4])
        subg = sb("subg", [P, P])
        negm = sb("negm", [P, 2, 2])
        sums = sb("sums", [P, 2, 2])
        rsum = sb("rsum", [P, HEADS])
        st = sb("st", [P, 2, 6])
        mv = sb("mv", [P, NT, 2])
        var = sb("var", [P, 8])
        newt = sb("newt", [P, 8])
        rstd = sb("rstd", [P, 8])
        gatew = sb("gatew", [P, 2, NT])
        sloti = sb("sloti", [P, 2 * NT], I32)
        rowi = sb("rowi", [BLK, NBX], I32)
        idy = sb("idy", [BLK, 1], I32)
        toki = sb("toki", [BLK, NBX], I32)
        idx = sb("idx", [BLK, 1], I32)
        tabi = sb("tabi", [1, T_N], I32)

        mrow, badb = overlay([("mrow", [2, LAYERS, 6 * D], F32), ("badb", [2, LAYERS, 6 * D], F32)])
        qkv, hT, qT, kT, kctx, vctx, o = overlay([
            ("qkv", [P, NT, 3 * D], F32), ("hT", [P, KD, NT * P], F32), ("qT", [P, KD, NT * P], F32),
            ("kT", [P, KD, 4 * P], F32), ("kctx", [P, D], F32), ("vctx", [P, D], F32), ("o", [P, NT, D], F32)])
        wh, wl = overlay([("wh", [P, RING, CH], F32R), ("wl", [P, RING, CH], F32R)])
        sb("large_region", [P, 2 * RING * CH])
        rope, t1 = overlay([("rope", [P, 4, 512], F32), ("t1", [P, D], F32)])
        (btab,) = overlay([("btab", [P, HEADS * BM * GRID_W], F32)])
        xs, hs, xg, gsb, usb, sg, hm, yl, yo = overlay([
            ("xs", [P, KD, 2 * BLK], F32R), ("hs", [P, 4, 2 * BLK], F32R), ("xg", [BLK, D], F32),
            ("gsb", [P, DE], F32), ("usb", [P, DE], F32), ("sg", [P, 4 * BLK], F32), ("hm", [P, 4 * BLK], F32),
            ("yl", [BLK, D], F32), ("yo", [BLK, D], F32)])
        sb("small_region", [P, 6144])

        hTf = hT[:, :, :].rearrange("p k n -> p (k n)")
        s_sb = hTf[:, 0:768].rearrange("p (h n) -> p h n", h=2)
        prob = [hTf[:, 768 * (1 + i):768 * (2 + i)].rearrange("p (h n) -> p h n", h=2) for i in range(2)]
        probT = hTf[:, 2304:3072].rearrange("p (h n) -> p h n", h=2)
        oT = qT
        lnb = kT[:, :, :].rearrange("p k n -> p (k n)").rearrange("p (v d) -> p v d", v=4)
        rt = kT[:, :, :].rearrange("p k n -> p (k n)")
        ypair = qkv[:, :, :].rearrange("p t n -> p (t n)").rearrange("p (s d) -> p s d", d=D)
        hank = o[:, :, :].rearrange("p t n -> p (t n)")

        ps_t = ctx.enter_context(nc.psum_tensor("ps", [P, 8 * 512], F32))
        ps = ps_t[:, :].rearrange("p (b n) -> p b n", b=8)

        def tile_ps(t):
            return ps_t[:, 1024 * t:1024 * (t + 1)]

        ident = cst[:, C_ID:C_ID + P]
        ident64 = cst[0:BLK, C_ID:C_ID + BLK]
        stack2 = cst[:, C_II:C_II + BLK]
        ones = cst[:, C_ONE:C_ONE + P]
        tri = cst[:, C_TRI:C_TRI + P]

        mdram = nc.dram_tensor("mdram", (LAYERS, 2, 6 * D), F32).ap()
        xmod = nc.dram_tensor("xmod", (NT * P, D), F32).ap()
        ybuf = nc.dram_tensor("ybuf", (TOPK * NT * P + BLK, D), F32).ap()
        bpad = nc.dram_tensor("bpad", (2, HEADS * BM, P), F32).ap()

        ld_small = sem("ld_small")
        ld_bada = sem("ld_bada")
        st_land = [sem(f"st_land{i}") for i in range(RING)]
        st_free = sem("st_free")
        cond_rdy = sem("cond_rdy")
        ada_evac = sem("ada_evac")
        mrow_saved = sem2("mrow_saved")
        mod_ld, mod_used, lnb_ld = sem("mod_ld"), sem("mod_used"), sem("lnb_ld")
        lam_rdy = sem("lam_rdy")
        pad_zero, pad_done = sem("pad_zero"), sem("pad_done")
        hank_ld, flip_done, flip_used = sem("hank_ld"), sem("flip_done"), sem("flip_used")
        out_done = sem("out_done")
        ctx_ld = sem2("ctx_ld")
        h_rdy, hT_ps, hT_rdy = sem2("h_rdy"), sem2("hT_ps"), sem2("hT_rdy")
        qkv_done, qkv_ev = sem2("qkv_done"), sem2("qkv_ev")
        roped = sem("roped")
        qk_ps, qT_ev, kT_ev = sem2("qk_ps"), sem2("qT_ev"), sem2("kT_ev")
        sc_done, negm_rdy, exp_done, comb_done = sem2("sc_done"), sem2("negm_rdy"), sem2("exp_done"), sem2("comb_done")
        pT_done, pT_ev, pv_done, o_ev, o_rdy = sem2("pT_done"), sem2("pT_ev"), sem2("pv_done"), sem2("o_ev"), sem2("o_rdy")
        oT_ps, oT_rdy = sem2("oT_ps"), sem2("oT_rdy")
        xm_rdy, xmod_w, xT_ps, xT_rdy = sem2("xm_rdy"), sem2("xmod_w"), sem2("xT_ps"), sem2("xT_rdy")
        rt_pe, rt_dve, rt_act = sem2("rt_pe"), sem2("rt_dve"), sem2("rt_act")
        tab_rdy, tok_rdy = sem2("tab_rdy"), sem2("tok_rdy")
        moe_land = [[sem(f"moe_land{l}_{i}") for i in range(RING)] for l in range(LAYERS)]
        gu_high, gu_used, dn_high, dn_used = sem2("gu_high"), sem2("gu_used"), sem2("dn_high"), sem2("dn_used")
        gu_rest, up_rest, dn_rest, dn2_rest = sem2("gu_rest"), sem2("up_rest"), sem2("dn_rest"), sem2("dn2_rest")
        idx_rdy, idy_rdy, gath, xg_used = sem2("idx_rdy"), sem2("idy_rdy"), sem2("gath"), sem2("xg_used")
        xsh_rdy, xsl_rdy = sem2("xsh_rdy"), sem2("xsl_rdy")
        g_rdy, u_rdy, gut_done, sg_rdy, hm_rdy = sem2("g_rdy"), sem2("u_rdy"), sem2("gut_done"), sem2("sg_rdy"), sem2("hm_rdy")
        hh_rdy, hl_rdy, yo_rdy, y_wr = sem2("hh_rdy"), sem2("hl_rdy"), sem2("yo_rdy"), sem2("y_wr")
        pool_steps, pe_steps = sem("pool_steps"), sem("pe_steps")
        yg_ld, x_rdy = sem2("yg_ld"), sem2("x_rdy")

        ADA = 48
        QKV0 = [ADA + 18 * l for l in range(LAYERS)]
        WO0 = [q + 12 for q in QKV0]
        w_qkv, w_o = [w_qkv_a, w_qkv_b], [w_o_a, w_o_b]
        keys = [P, 3 * P, 3 * P]
        key0 = [0, P, P]
        UNITS = NT * PAIRS

        def wait_chunk(eng, n):
            eng.wait_ge(st_land[n % RING], 16 * (n // RING + 1))

        def table(eng, col, lo, hi):
            return eng.value_load(tabi[0:1, bass.ds(col, 1)] if not isinstance(col, int) else tabi[0:1, col:col + 1],
                                  min_val=lo, max_val=hi)

        def wait_apart(eng, step, s, value):
            eng.wait_ge(s, value)
            eng.sem_inc(step, 1)

        def high(l, s, e):
            return (gu_high[l], e * GU + s + 1) if s < GU else (dn_high[l], e * DN + (s - GU + 1))

        def rest(l, s, e):
            if s < 3:
                return gu_rest[l], e * 3 + (s + 4)
            return (up_rest, dn_rest, dn2_rest)[s - 3][l], e + 2

        def chunk_use(l, s, b):
            return (gu_used[l], b * GU + (s + 1 - GU)) if s < GU else (dn_used[l], b * DN + (s + 1 - GU - DN))

        def rests(eng, unit, l, b, ordn, chunks):
            for s in chunks:
                eng.wait_ge(*high(l, s, ordn))
                if not (isinstance(b, int) and b == 0):
                    eng.wait_ge(*chunk_use(l, s, b))
                unit.tensor_tensor(wl[:, s, :], raw[:, s, :], wh[:, s, :].bitcast(F32), ALU.subtract)\
                    .then_inc((gu_rest, gu_rest, gu_rest, up_rest, dn_rest, dn2_rest)[s][l], 1)

        block = ctx.enter_context(nc.Block())

        @block.sync
        def _(sp):
            def taken(l, s, i):
                if s < 3:
                    return gu_rest[l], i * 3 + (s + 1)
                return (up_rest, dn_rest, dn2_rest)[s - 3][l], i + 1

            with sp.Fori(0, LAYERS) as l:
                with sp.Fori(0, 4) as m:
                    for s in range(RING):
                        col = m * 1536 + (s // 2) * 512
                        sp.wait_ge(st_free, (l * 4 + m) * RING + s + 1)
                        sp.dma_start(
                            raw[:, s, :].rearrange("p (k n) -> p k n", k=4),
                            w_ada[bass.ds(l, 1), :, bass.ds(col, 512)].rearrange("a (p k) n -> p (a k) n", k=KD)
                            [:, 4 * (s % 2):4 * (s % 2) + 4, :]).then_inc(st_land[s], 16)
            for l in range(LAYERS):
                wq = w_qkv[l].rearrange("a (p k) n -> p (a k) n", k=KD)
                for cidx in range(12):
                    n = QKV0[l] + cidx
                    g, ck = cidx // 4, cidx % 4
                    if l and cidx < RING:
                        sp.wait_ge(*taken(l - 1, cidx, n_act))
                    else:
                        sp.wait_ge(st_free, n + 1)
                    sp.dma_start(raw[:, n % RING, :].rearrange("p (k n) -> p k n", k=2),
                                 wq[:, 2 * ck:2 * ck + 2, g * D:(g + 1) * D]).then_inc(st_land[n % RING], 16)
                wo = w_o[l].rearrange("a (p k) n -> p (a k) n", k=KD)
                k = 0
                for cidx, nk in enumerate(WO_K):
                    n = WO0[l] + cidx
                    sp.wait_ge(st_free, n + 1)
                    sp.dma_start(raw[:, n % RING, 0:nk * D].rearrange("p (k n) -> p k n", k=nk),
                                 wo[:, k:k + nk, :]).then_inc(st_land[n % RING], 16)
                    k += nk

                sp.wait_ge(tab_rdy[l], 1)
                n_act = table(sp, T_NACT, 2, NE)

                def load(i, chunks):
                    e = table(sp, T_LIST + i, 0, NE - 1)
                    for s in chunks:
                        if s >= GU or isinstance(i, int):
                            sp.wait_ge(st_free, WO0[l] + RING + s + 1)
                        if not isinstance(i, int):
                            sp.wait_ge(*taken(l, s, i))
                        w = (w_gate, w_up, w_down)[s // 2]
                        src = w[l, bass.ds(e, 1)]
                        kk = KD if s < GU else 4
                        part = kk // 2
                        src = src.rearrange("a (p k) n -> p (a k) n", k=kk)[:, part * (s % 2):part * (s % 2 + 1), :]
                        sp.dma_start(raw[:, s, :].rearrange("p (k n) -> p k n", k=part), src).then_inc(moe_land[l][s], 16)

                load(0, range(GU))
                with sp.Fori(1, n_act) as i:
                    load(i, range(2))
                    load(i - 1, range(GU, RING))
                    load(i, range(2, GU))
                load(n_act - 1, range(GU, RING))

        @block.gpsimd
        def _(pool):
            for hf in range(2):
                pool.dma_start(bpad[hf], consts[0:HEADS * BM, C_ZERO:C_ZERO + P]).then_inc(pad_zero, 16)
            pool.wait_ge(pad_zero, 32)
            for hf in range(2):
                pool.dma_start(bpad[hf].rearrange("(h m) n -> h m n", m=BM)[:, :, 48:48 + 2 * NA_KW - 1],
                               rpb_b[0, :, 5 - hf:5 - hf + BM, :]).then_inc(pad_done, 16)

            def rows(l, cnd, vec):
                return mdram[l, cnd:cnd + 1, vec * D:(vec + 1) * D].to_broadcast([P, D])

            def load_mod(l, stage):
                for cnd in range(2):
                    for i, vec in enumerate((3 * stage + 1, 3 * stage)):
                        pool.dma_start(modb[:, 2 * cnd + i, :], rows(l, cnd, vec)).then_inc(mod_ld, 16)

            def load_ln(l, stage):
                for cnd in range(2):
                    pool.dma_start(lnb[:, cnd, :], rows(l, cnd, 3 * stage + 2)).then_inc(lnb_ld, 16)
                for i, w in enumerate((ln_g, ln_b)):
                    pool.dma_start(lnb[:, 2 + i, :], w[l, stage:stage + 1, :].to_broadcast([P, D])).then_inc(lnb_ld, 16)

            for l in range(LAYERS):
                pool.wait_ge(ada_evac, 3 + 12 * (l + 1))
                pool.dma_start(mdram[l], mrow[:, l, :]).then_inc(mrow_saved[l], 16)
            for l in range(LAYERS):
                pool.wait_ge(mrow_saved[l], 16)
            load_mod(0, 0)

            for l in range(LAYERS):
                ck, cv = ((cache_a_k, cache_a_v), (cache_b_k, cache_b_v))[l]
                pool.dma_start(kctx[:, :], ck[0, 0].rearrange("t h d -> t (h d)")).then_inc(ctx_ld[l], 16)
                pool.dma_start(vctx[:, :], cv[0, 0].rearrange("t h d -> t (h d)")).then_inc(ctx_ld[l], 16)
                if l == 1:
                    for r in range(2):
                        if r:
                            pool.wait_ge(flip_done, 6)
                        for hf in range(2):
                            src = bass.AP(tensor=bpad.tensor, offset=(hf * HEADS * BM + r * 8 * BM) * P,
                                          ap=[[1, 64], [P, 8 * BM], [1, GRID_W]])
                            if r == 0 and hf == 0:
                                pool.wait_ge(pad_done, 32)
                                pool.wait_ge(x_rdy[0], NT)
                            pool.dma_start(hank[64 * hf:64 * hf + 64, :].rearrange("p (a n) -> p a n", n=GRID_W),
                                           src).then_inc(hank_ld, 16)
                nk, nv = ((new_a_k, new_a_v), (new_b_k, new_b_v))[l]
                pool.wait_ge(qkv_ev[l], 6)
                pool.dma_start(nk[0, 0].rearrange("t h d -> t (h d)"), qkv[:, 0, D:2 * D]).then_inc(out_done, 16)
                pool.wait_ge(qkv_ev[l], 9)
                pool.dma_start(nv[0, 0].rearrange("t h d -> t (h d)"), qkv[:, 0, 2 * D:3 * D]).then_inc(out_done, 16)
                pool.wait_ge(mod_used, 2 * l + 1)
                load_mod(l, 1)
                pool.wait_ge(pv_done[l], UNITS)
                load_ln(l, 0)
                pool.wait_ge(xm_rdy[l], NT)
                pool.dma_start(xmod.rearrange("(t p) d -> p t d", p=P), qkv[:, :, 0:D]).then_inc(xmod_w[l], 16)

                pool.wait_ge(tok_rdy[l], 1)
                pool.wait_ge(tab_rdy[l], 1)
                n_blk = table(pool, T_NBLK, 12, NB)
                pool.wait_ge(xmod_w[l], 16)
                pool.wait_ge(out_done, 32 * (l + 1))

                def gather(b):
                    pool.tensor_copy(idx[:, :], toki[:, bass.ds(b, 1)] if not isinstance(b, int) else toki[:, b:b + 1])\
                        .then_inc(idx_rdy[l], 1)
                    wait_apart(pool, pool_steps, idx_rdy[l], b + 1)
                    pool.indirect_dma_start(out=xg[:, :], out_offset=None, in_=xmod,
                                            in_offset=bass.IndirectOffsetOnAxis(ap=idx[:, 0:1], axis=0))\
                        .then_inc(gath[l], 16)

                def store(b):
                    wait_apart(pool, pool_steps, yo_rdy[l], b + 2)
                    pool.tensor_copy(idy[:, :], rowi[:, bass.ds(b, 1)]).then_inc(idy_rdy[l], 1)
                    wait_apart(pool, pool_steps, idy_rdy[l], b + 1)
                    pool.indirect_dma_start(out=ybuf, out_offset=bass.IndirectOffsetOnAxis(ap=idy[:, 0:1], axis=0),
                                            in_=yo[:, :], in_offset=None).then_inc(y_wr[l], 16)

                def next_gather(b):
                    pool.wait_ge(xg_used[l], b + 1)
                    pool.wait_ge(gath[l], (b + 1) * 16)
                    gather(b + 1)

                def split_ahead(b):
                    ord_next = table(pool, T_ORD + 1 + b, 0, NE - 1)
                    first_next = table(pool, T_FIRST + 1 + b, 0, 1)
                    with pool.If(first_next > 0):
                        rests(pool, nc.gpsimd, l, b + 1, ord_next, [3])

                def split_own(b):
                    ordn = table(pool, T_ORD + b, 0, NE - 1)
                    first = table(pool, T_FIRST + b, 0, 1)
                    with pool.If(first > 0):
                        rests(pool, nc.gpsimd, l, b, ordn, [5])

                gather(0)
                rests(pool, nc.gpsimd, l, 0, 0, [3])
                next_gather(0)
                rests(pool, nc.gpsimd, l, 0, 0, [5])
                next_gather(1)
                split_ahead(0)
                with pool.Fori(1, n_blk) as b:
                    split_own(b)
                    next_gather(b + 1)
                    store(b - 1)
                    split_ahead(b)
                store(table(pool, T_LAST, 11, NB - 1))
                wait_apart(pool, pool_steps, gath[l], n_blk * 16 + 32)
                wait_apart(pool, pool_steps, y_wr[l], n_blk * 16)
                load_ln(l, 1)
                pool.dma_start(ypair[:, 0:2 * NT, :], ybuf[0:2 * NT * P, :].rearrange("(s p) d -> p s d", p=P))\
                    .then_inc(yg_ld[l], 16)
                if l == 0:
                    pool.wait_ge(mod_used, 2)
                    load_mod(1, 0)
                    pool.wait_ge(x_rdy[0], NT)
            for t in range(NT):
                pool.wait_ge(x_rdy[1], t + 1)
                dst = y_prompt[0] if t == 0 else y_sample[0, (t - 1) * P:t * P, :]
                pool.dma_start(dst, x[:, t, :]).then_inc(out_done, 16)
            pool.wait_ge(out_done, 16 * (4 + NT))

        @block.scalar
        def _(act):
            small = 0

            def load(dst, src):
                nonlocal small
                act.dma_start(dst, src).then_inc(ld_small, 16)
                small += 16

            load(condr[:, 0, :], c_ctx.rearrange("(p k) -> p k", k=KD))
            load(condr[:, 1, :], c[0].rearrange("(p k) -> p k", k=KD))
            load(cst[:, :], consts)
            act.wait_ge(ld_small, small)
            act.activation(cond[:, :, :].rearrange("p k c -> p c k"), condr[:, :, :], ACT.Silu).then_inc(cond_rdy, 1)
            for l in range(LAYERS):
                act.dma_start(badb[:, l, :], b_ada[l:l + 1, :].to_broadcast([2, 6 * D])).then_inc(ld_bada, 16)
            load(x[:, 0, :], x_prompt[0])
            load(x[:, 1:3, :], x_sample[0].rearrange("(t p) d -> p t d", p=P))
            for l in range(LAYERS):
                load(wr[:, l, :, 0:NG], w_rg[l].rearrange("(p k) n -> p k n", k=KD))
                load(wr[:, l, :, NG:], w_re[l].rearrange("(p k) n -> p k n", k=KD))
                load(br[:, l, 0:NG], b_rg[l:l + 1, :].to_broadcast([P, NG]))
                load(br[:, l, NG:], b_re[l:l + 1, :].to_broadcast([P, NE]))
            load(lamb[:, :], lam_a.rearrange("a f d -> a (f d)").to_broadcast([P, 4 * HD]))
            load(subg[:, :], subln_a.to_broadcast([P, P]))
            act.wait_ge(lam_rdy, 1)
            act.activation(lam[:, 2:4], lam[:, 0:2], ACT.Exp).then_inc(lam_rdy, 1)

            def take_transposed(dst, done, ready):
                for t in range(NT):
                    act.wait_ge(done, t + 1)
                    act.activation(dst[:, :, t * P:(t + 1) * P], tile_ps(t).rearrange("p (k n) -> p k n", k=KD),
                                   ACT.Copy).then_inc(ready, 1)

            for l in range(LAYERS):
                take_transposed(hT, hT_ps[l], hT_rdy[l])
                for g in range(3):
                    for t in range(NT):
                        if t < NT - 1:
                            act.wait_ge(qkv_done[l], 2 * g + t + 1)
                        else:
                            act.wait_ge(st_free, RING + QKV0[l] + 4 * (g + 1))
                        act.activation(qkv[:, t, g * D:(g + 1) * D], tile_ps(t), ACT.Copy).then_inc(qkv_ev[l], 1)
                for j in range(PAIRS):
                    act.wait_ge(qk_ps[l], 2 * j + 1)
                    act.activation(qT[:, j, :], ps[:, 4 + 2 * (j % 2), 0:NT * P], ACT.Copy).then_inc(qT_ev[l], 1)

                def exps(u):
                    t = u // PAIRS
                    n = keys[t]
                    e = prob[u % 2]
                    act.wait_ge(negm_rdy[l], u + 1)
                    if u >= 2:
                        act.wait_ge(pT_done[l], u - 1)
                    for h in range(2):
                        src = ps[:, 2 * (u % 2) + h, 0:n] if l == 0 else s_sb[:, h, 0:n]
                        ins = act.activation(e[:, h, 0:n], src, ACT.Exp, bias=negm[:, u % 2, h:h + 1],
                                             scale=SCALE if l == 0 else 1.0, accum_out=sums[:, u % 2, h:h + 1])
                    ins.then_inc(exp_done[l], 1)

                def take_pT(u):
                    n = keys[u // PAIRS]
                    act.wait_ge(pT_done[l], u + 1)
                    if u:
                        act.wait_ge(pv_done[l], u)
                    if l == 0:
                        act.activation(probT[:, 0, 0:n], ps[:, 4 + u % 2, 0:n], ACT.Copy).then_inc(pT_ev[l], 1)
                    else:
                        act.activation(probT[:, :, 0:n], ps[:, 4:6, 0:n], ACT.Copy).then_inc(pT_ev[l], 1)
                    if l == 0 and u % PAIRS == PAIRS - 1:
                        act.wait_ge(pv_done[l], u + 1)
                        act.activation(o[:, u // PAIRS, :], tile_ps(3), ACT.Copy).then_inc(o_ev[l], 1)

                for u in range(UNITS):
                    exps(u)
                    if u:
                        take_pT(u - 1)
                take_pT(UNITS - 1)
                take_transposed(oT, oT_ps[l], oT_rdy[l])
                take_transposed(hT, xT_ps[l], xT_rdy[l])
                rx = rt[:, 64:64 + 15]
                act.wait_ge(rt_dve[l], 1)
                act.activation(rx, rx, ACT.Exp).then_inc(rt_act[l], 1)

                act.wait_ge(tab_rdy[l], 1)
                n_blk = table(act, T_NBLK, 12, NB)

                def split_high(b, ordn, chunks):
                    for s in chunks:
                        act.wait_ge(moe_land[l][s], (ordn + 1) * 16)
                        if not (isinstance(b, int) and b == 0):
                            act.wait_ge(*chunk_use(l, s, b))
                        act.activation(wh[:, s, :], raw[:, s, :], ACT.Copy).then_inc(gu_high[l] if s < GU else dn_high[l], 1)

                def x_high(b):
                    act.wait_ge(xg_used[l], b + 1)
                    act.activation(xs[:, :, 0:BLK], ps[:, 0, :].rearrange("p (k n) -> p k n", k=KD), ACT.Copy)\
                        .then_inc(xsh_rdy[l], 1)

                def hidden(b):
                    act.wait_ge(gut_done[l], b * 2 + 1)
                    if not (isinstance(b, int) and b == 0):
                        act.wait_ge(hm_rdy[l], b)
                    act.activation(sg[:, :], ps[:, 3, 0:4 * BLK], ACT.Silu).then_inc(sg_rdy[l], 1)
                    act.wait_ge(hm_rdy[l], b + 1)
                    act.activation(hs[:, :, 0:BLK], hm[:, :].rearrange("p (k n) -> p k n", k=4), ACT.Copy)\
                        .then_inc(hh_rdy[l], 1)

                def body(b):
                    later = not isinstance(b, int)
                    act.wait_ge(*chunk_use(l, 1, b + 1))
                    if later:
                        act.wait_ge(gut_done[l], b * 2 - 1)
                    act.activation(gsb[:, :], ps[:, 1, :], ACT.Copy).then_inc(g_rdy[l], 1)
                    ord_next = table(act, T_ORD + 1 + b, 0, NE - 1)
                    first_next = table(act, T_FIRST + 1 + b, 0, 1)
                    with act.If(first_next > 0):
                        split_high(b + 1, ord_next, range(2))
                    if later:
                        ordn = table(act, T_ORD + b, 0, NE - 1)
                        first = table(act, T_FIRST + b, 0, 1)
                        with act.If(first > 0):
                            split_high(b, ordn, [4])
                    else:
                        split_high(b, 0, [4])
                    act.wait_ge(*chunk_use(l, 3, b + 1))
                    if later:
                        act.wait_ge(gut_done[l], b * 2)
                    act.activation(usb[:, :], ps[:, 2, :], ACT.Copy).then_inc(u_rdy[l], 1)
                    if later:
                        with act.If(first > 0):
                            split_high(b, ordn, [5])
                    else:
                        split_high(b, 0, [5])
                    x_high(b + 1)
                    hidden(b)
                    with act.If(first_next > 0):
                        split_high(b + 1, ord_next, range(2, GU))

                act.wait_ge(xmod_w[l], 16)
                act.wait_ge(rt_dve[l], 1)
                split_high(0, 0, range(GU))
                x_high(0)
                body(0)
                with act.Fori(1, n_blk) as b:
                    body(b)

        @block.tensor
        def _(pe):
            mm = nc.tensor.matmul
            pe.sem_inc(st_free, RING)
            pe.wait_ge(cond_rdy, 1)
            with pe.Fori(0, LAYERS) as l:
                with pe.Fori(0, 4) as m:
                    it = l * 4 + m
                    for s in range(RING):
                        pe.wait_ge(st_land[s], (it + 1) * 16)
                        if s % 2 == 0:
                            pe.wait_ge(ada_evac, it * 3 + s // 2 + 1)
                        for kk in range(4):
                            k = 4 * (s % 2) + kk
                            ins = mm(ps[0:2, s // 2, :], cond[:, k, :], raw[:, s, kk * 512:(kk + 1) * 512],
                                     start=(k == 0), stop=(k == KD - 1))
                        ins.then_inc(st_free, 1)

            def transpose_tiles(src, ready, done):
                for t in range(NT):
                    pe.wait_ge(ready, t + 1)
                    for k in range(KD):
                        ins = nc.tensor.transpose(tile_ps(t)[:, k * P:(k + 1) * P],
                                                  src(t).rearrange("p (c k) -> p k c", k=KD)[:, k, :], ident)
                    ins.then_inc(done, 1)

            def project(lhs, nk, k0, slot, last, tile_done):
                for kk in range(nk):
                    k = k0 + kk
                    for t in range(NT):
                        for hf in range(2):
                            ins = mm(ps[:, 2 * t + hf, :], lhs[:, k, t * P:(t + 1) * P],
                                     raw[:, slot, kk * D + hf * 512:kk * D + (hf + 1) * 512],
                                     start=(k == 0), stop=(k == KD - 1))
                        if tile_done is not None and last and kk == nk - 1 and t < NT - 1:
                            ins.then_inc(tile_done, 1)
                ins.then_inc(st_free, 1)

            for l in range(LAYERS):
                transpose_tiles(lambda t: qkv[:, t, 0:D], h_rdy[l], hT_ps[l])
                pe.wait_ge(hT_rdy[l], NT)
                for g in range(3):
                    if g:
                        pe.wait_ge(qkv_ev[l], 3 * g)
                    for ck in range(4):
                        n = QKV0[l] + 4 * g + ck
                        wait_chunk(pe, n)
                        project(hT, 2, 2 * ck, n % RING, ck == 3, qkv_done[l])
                    if l == 1 and g < 2:
                        pe.wait_ge(hank_ld, 32 * (g + 1))
                        for i in range(6):
                            f = 6 * g + i
                            if f >= 2:
                                pe.wait_ge(flip_used, f - 1)
                            mm(ps[:, 6 + f % 2, :], cst[:, C_FLIP:C_FLIP + P], hank[:, i * 512:(i + 1) * 512],
                               start=True, stop=True).then_inc(flip_done, 1)
                if l == 0:
                    pe.wait_ge(roped, 4)
                else:
                    pe.wait_ge(flip_used, 12)
                pe.wait_ge(qkv_ev[l], 9)
                pe.wait_ge(ctx_ld[l], 32)
                for j in range(PAIRS):
                    bq, bk = 4 + 2 * (j % 2), 5 + 2 * (j % 2)
                    if j >= 2:
                        pe.wait_ge(qT_ev[l], j - 1)
                        pe.wait_ge(kT_ev[l], j - 1)
                    for t in range(NT):
                        ins = nc.tensor.transpose(ps[:, bq, t * P:(t + 1) * P], qkv[:, t, j * P:(j + 1) * P], ident)
                    ins.then_inc(qk_ps[l], 1)
                    kin = [qkv[:, 0, D + j * P:D + (j + 1) * P], kctx[:, j * P:(j + 1) * P],
                           qkv[:, 1, D + j * P:D + (j + 1) * P], qkv[:, 2, D + j * P:D + (j + 1) * P]]
                    for i in range(4):
                        ins = nc.tensor.transpose(ps[:, bk, i * P:(i + 1) * P], kin[i], ident)
                    ins.then_inc(qk_ps[l], 1)
                pe.wait_ge(qT_ev[l], PAIRS)
                pe.wait_ge(kT_ev[l], PAIRS)

                def values(t, i, lo, hi):
                    if t == 0:
                        return qkv[:, 0, 2 * D + lo:2 * D + hi]
                    return vctx[:, lo:hi] if i == 0 else qkv[:, i, 2 * D + lo:2 * D + hi]

                def scores(u):
                    t, j = u // PAIRS, u % PAIRS
                    if u >= 2:
                        pe.wait_ge(exp_done[l] if l == 0 else negm_rdy[l], u - 1)
                    for h in range(2):
                        ins = mm(ps[:, 2 * (u % 2) + h, 0:keys[t]],
                                 qT[HD * h:HD * (h + 1), j, t * P:(t + 1) * P],
                                 kT[HD * h:HD * (h + 1), j, key0[t]:key0[t] + keys[t]], start=True, stop=True)
                    ins.then_inc(sc_done[l], 1)

                def attend(u):
                    t, j = u // PAIRS, u % PAIRS
                    nk = keys[t] // P
                    maps = 1 if l == 0 else 2
                    pe.wait_ge(comb_done[l] if l == 0 else exp_done[l], u + 1)
                    if u >= (2 if l == 0 else 1):
                        pe.wait_ge(pT_ev[l], u - 1 if l == 0 else u)
                    for h in range(maps):
                        for i in range(nk):
                            ins = nc.tensor.transpose(ps[:, 4 + (u % 2 if l == 0 else h), i * P:(i + 1) * P],
                                                      prob[u % 2][:, h, i * P:(i + 1) * P], ident)
                    ins.then_inc(pT_done[l], 1)
                    pe.wait_ge(pT_ev[l], u + 1)
                    if j == 0 and t:
                        pe.wait_ge(o_ev[l], t)
                    w = P // maps
                    for h in range(maps):
                        lo = j * P + h * w
                        for i in range(nk):
                            ins = mm(tile_ps(3)[:, lo:lo + w], probT[:, h, i * P:(i + 1) * P], values(t, i, lo, lo + w),
                                     start=(i == 0), stop=(i == nk - 1))
                    ins.then_inc(pv_done[l], 1)

                scores(0)
                for u in range(UNITS):
                    if u + 1 < UNITS:
                        scores(u + 1)
                    attend(u)

                transpose_tiles(lambda t: o[:, t, :], o_rdy[l], oT_ps[l])
                pe.wait_ge(oT_rdy[l], NT)
                k = 0
                for cidx, nk in enumerate(WO_K):
                    n = WO0[l] + cidx
                    wait_chunk(pe, n)
                    project(oT, nk, k, n % RING, False, None)
                    k += nk

                transpose_tiles(lambda t: qkv[:, t, 0:D], xm_rdy[l], xT_ps[l])
                pe.wait_ge(xT_rdy[l], NT)
                w36 = NG + NE
                for t in range(NT):
                    for k in range(KD):
                        ins = mm(ps[:, 6, t * w36:(t + 1) * w36], hT[:, k, t * P:(t + 1) * P], wr[:, l, k, :],
                                 start=(k == 0), stop=(k == KD - 1))
                ins.then_inc(rt_pe[l], 1)
                pe.wait_ge(rt_dve[l], 2)
                a_all = rt[:, 384:480].rearrange("p (t e) -> p t e", t=NT)
                for t in range(NT):
                    for i in range(t + 1):
                        mm(ps[:, 7, t * NE:(t + 1) * NE], tri if i == t else ones, a_all[:, i, :],
                           start=(i == 0), stop=(i == t))
                for t in range(NT):
                    ins = mm(ps[0:NE, 5, 0:1], a_all[:, t, :], ones[:, 0:1], start=(t == 0), stop=(t == NT - 1))
                ins.then_inc(rt_pe[l], 1)
                pe.wait_ge(rt_dve[l], 3)
                mm(ps[0:NE, 4, 0:2], tri[0:NE, 0:NE], rt[0:NE, 600:602], start=True, stop=True)
                mm(ps[:, 3, 0:NE], rt[0:NE, 640:768], tri[0:NE, 0:NE], start=True, stop=True).then_inc(rt_pe[l], 1)
                pe.wait_ge(rt_dve[l], 4)
                mm(ps[0:1, 2, T_LIST:T_LIST + NE], cst[0:NE, C_TOK:C_TOK + 1], rt[0:NE, 800:832], start=True, stop=True)
                mm(ps[0:1, 2, T_ORD:T_ORD + 48], rt[0:NE, 605:606], rt[0:NE, 832:880], start=True, stop=True)
                mm(ps[0:1, 2, T_FIRST:T_FIRST + 48], rt[0:NE, 601:602], rt[0:NE, 880:928], start=True, stop=True)
                mm(ps[0:1, 2, T_NACT:T_NACT + 1], rt[0:NE, 601:602], ones[0:NE, 0:1], start=True, stop=True)
                mm(ps[0:1, 2, T_NBLK:T_NBLK + 1], rt[0:NE, 600:601], ones[0:NE, 0:1], start=True, stop=True)\
                    .then_inc(rt_pe[l], 1)
                pe.wait_ge(rt_dve[l], 5)
                for i in range(2 * NT):
                    ins = mm(ps[0:BLK, 1, 0:NBX], rt[:, 1200 + i * BLK:1200 + (i + 1) * BLK],
                             rt[:, 1600 + i * NBX:1600 + (i + 1) * NBX], start=(i == 0), stop=(i == 2 * NT - 1))
                ins.then_inc(rt_pe[l], 1)

                pe.wait_ge(tab_rdy[l], 1)
                pe.wait_ge(tok_rdy[l], 1)
                n_blk = table(pe, T_NBLK, 12, NB)

                def transpose_x(b):
                    wait_apart(pe, pe_steps, gath[l], (b + 1) * 16)
                    for k in range(KD):
                        ins = nc.tensor.transpose(ps[:, 0, k * BLK:(k + 1) * BLK],
                                                  xg[:, :].rearrange("p (c k) -> p k c", k=KD)[:, k, :], ident64)
                    ins.then_inc(xg_used[l], 1)

                def gate_or_up(b, ordn, i):
                    for s in range(2 * i, 2 * i + 2):
                        pe.wait_ge(*high(l, s, ordn))
                        pe.wait_ge(*rest(l, s, ordn))
                        if s % 2 == 0 and not isinstance(b, int):
                            pe.wait_ge((g_rdy, u_rdy)[i][l], b)
                        for kk in range(4):
                            k = 4 * (s % 2) + kk
                            for part in (wh, wl):
                                ins = mm(ps[:, 1 + i, :], xs[:, k, :], part[:, s, kk * 512:(kk + 1) * 512],
                                         start=(k == 0 and part is wh), stop=(k == KD - 1 and part is wl))
                        ins.then_inc(gu_used[l], 1)

                def down(b, ordn):
                    pe.wait_ge(hh_rdy[l], b + 1)
                    pe.wait_ge(hl_rdy[l], b + 1)
                    pe.wait_ge(yo_rdy[l], b + 1)
                    for s in range(GU, RING):
                        pe.wait_ge(*high(l, s, ordn))
                        pe.wait_ge(*rest(l, s, ordn))
                        for jj in range(2):
                            j = 2 * (s - GU) + jj
                            for hf in range(2):
                                for part in (wh, wl):
                                    ins = mm(ps[:, 5 + hf, :], hs[:, j, :],
                                             part[:, s, jj * D + hf * 512:jj * D + (hf + 1) * 512],
                                             start=(j == 0 and part is wh), stop=(j == 3 and part is wl))
                        ins.then_inc(dn_used[l], 1)

                def body(b):
                    later = not isinstance(b, int)
                    ordn = table(pe, T_ORD + b, 0, NE - 1) if later else 0
                    pe.wait_ge(xsh_rdy[l], b + 1)
                    pe.wait_ge(xsl_rdy[l], b + 1)
                    gate_or_up(b, ordn, 0)
                    if later:
                        down(b - 1, table(pe, T_ORD - 1 + b, 0, NE - 1))
                    gate_or_up(b, ordn, 1)
                    for i, (src, ready) in enumerate(((gsb, g_rdy), (usb, u_rdy))):
                        pe.wait_ge(ready[l], b + 1)
                        if later:
                            pe.wait_ge((sg_rdy, hm_rdy)[i][l], b)
                        for j in range(4):
                            ins = mm(ps[:, 3 + i, j * BLK:(j + 1) * BLK],
                                     src[:, :].rearrange("p (c j) -> p j c", j=4)[:, j, :], stack2, start=True, stop=True)
                        ins.then_inc(gut_done[l], 1)
                        if i == 0:
                            transpose_x(b + 1)

                transpose_x(0)
                body(0)
                with pe.Fori(1, n_blk) as b:
                    body(b)
                last_blk = table(pe, T_LAST, 11, NB - 1)
                down(last_blk, table(pe, T_ORD + last_blk, 0, NE - 1))

        @block.vector
        def _(dve):
            v = nc.vector

            def chain(ins):
                dve.drain()
                return ins

            dve.sem_inc(ada_evac, 3)
            for l in range(LAYERS):
                dve.sem_inc(yo_rdy[l], 1)
                dve.sem_inc(gu_rest[l], 3)
                for s in (up_rest, dn_rest, dn2_rest):
                    dve.sem_inc(s[l], 1)
            dve.wait_ge(ld_bada, 16 * LAYERS)
            with dve.Fori(0, LAYERS) as l:
                with dve.Fori(0, 4) as m:
                    it = l * 4 + m
                    for i in range(3):
                        dve.wait_ge(st_free, it * RING + RING + 2 * i + 2)
                        at = bass.ds(m * 1536 + i * 512, 512)
                        v.tensor_tensor(mrow[:, bass.ds(l, 1), at].rearrange("p a n -> p (a n)"), ps[0:2, i, :],
                                        badb[:, bass.ds(l, 1), at].rearrange("p a n -> p (a n)"),
                                        ALU.add).then_inc(ada_evac, 1)

            dve.wait_ge(ld_small, 16 * (3 + 2 + 4 * LAYERS + 2))
            lv = lamb[:, :].rearrange("p (a b d) -> p a b d", a=2, b=2)
            chain(v.tensor_tensor(lv[:, :, 0, :], lv[:, :, 0, :], lv[:, :, 1, :], ALU.mult))
            v.tensor_reduce(lam[:, 0:2], lv[:, :, 0, :], AX, ALU.add).then_inc(lam_rdy, 1)
            chain(v.tensor_scalar(subg[:, :], subg[:, :], 1.0 - LAM_INIT, None, ALU.mult))
            dve.wait_ge(lam_rdy, 2)
            chain(v.tensor_tensor(lam[:, 0:1], lam[:, 2:3], lam[:, 3:4], ALU.subtract))
            chain(v.tensor_scalar(lam[:, 0:1], lam[:, 0:1], LAM_INIT, None, ALU.add))

            def modulate(l, stage, ready):
                dve.wait_ge(mod_ld, 64 * (2 * l + stage + 1))
                for t in range(NT):
                    sc = 0 if t == 0 else 2
                    chain(v.scalar_tensor_tensor(qkv[:, t, 0:D], modb[:, sc, :], 1.0, x[:, t, :], ALU.add, ALU.mult))
                    v.tensor_tensor(qkv[:, t, 0:D], qkv[:, t, 0:D], modb[:, sc + 1, :], ALU.add).then_inc(ready, 1)
                dve.drain()
                dve.sem_inc(mod_used, 1)

            def rsqrt(r, a, tmp):
                ri = r.bitcast(I32)
                chain(v.tensor_single_scalar(ri, a.bitcast(I32), 1, op=ALU.arith_shift_right))
                chain(v.tensor_scalar(ri, ri, -1.0, float(0x5F3759DF), ALU.mult, ALU.add))
                for _ in range(4):
                    chain(v.tensor_tensor(tmp, r, r, ALU.mult))
                    chain(v.tensor_tensor(tmp, tmp, a, ALU.mult))
                    chain(v.tensor_scalar(tmp, tmp, -0.5, 1.5, ALU.mult, ALU.add))
                    chain(v.tensor_tensor(r, r, tmp, ALU.mult))

            def layer_norm(l, stage, src):
                dve.wait_ge(lnb_ld, 64 * (2 * l + stage + 1))
                for t in range(NT):
                    chain(v.tensor_tensor(t1[:, :], src(t), lnb[:, 0 if t == 0 else 1, :], ALU.mult))
                    chain(v.scalar_tensor_tensor(x[:, t, :], x[:, t, :], ALPHA, t1[:, :], ALU.mult, ALU.add))
                    for i in range(2):
                        v.bn_stats(st[:, i, :], x[:, t, i * 512:(i + 1) * 512])
                    dve.drain()
                    chain(v.bn_aggr(mv[:, t, :], st[:, :, :].rearrange("p a b -> p (a b)")))
                chain(v.tensor_scalar(var[:, 0:NT], mv[:, :, 1], EPS, None, ALU.add))
                rsqrt(rstd[:, 0:NT], var[:, 0:NT], newt[:, 0:NT])
                for t in range(NT):
                    chain(v.tensor_scalar(x[:, t, :], x[:, t, :], mv[:, t, 0:1], rstd[:, t:t + 1], ALU.subtract, ALU.mult))
                    chain(v.tensor_tensor(x[:, t, :], x[:, t, :], lnb[:, 2, :], ALU.mult))
                    chain(v.tensor_tensor(x[:, t, :], x[:, t, :], lnb[:, 3, :], ALU.add))
                    if stage == 1:
                        dve.sem_inc(x_rdy[l], 1)

            for l in range(LAYERS):
                if l == 0:
                    for i in range(LAYERS):
                        dve.wait_ge(mrow_saved[i], 16)
                modulate(l, 0, h_rdy[l])
                if l == 0:
                    for g in range(2):
                        dve.wait_ge(qkv_ev[l], 3 * (g + 1))
                        for t in range(1, NT):
                            hv = qkv[:, t, g * D:(g + 1) * D].rearrange("p (h a b j) -> p h a b j", a=2, b=2, j=16)\
                                .rearrange("p h a b j -> p (h a) b j")
                            tb = C_ROPE + (t - 1) * 64
                            cosb = cst[:, tb:tb + 32].unsqueeze(1).to_broadcast([P, HEADS, 32])\
                                .rearrange("p h (a j) -> p h a j", a=2)
                            sinb = cst[:, tb + 32:tb + 64].unsqueeze(1).to_broadcast([P, HEADS, 32])\
                                .rearrange("p h (a j) -> p h a j", a=2)
                            x1, x2 = (hv[:, :, b, :].rearrange("p (h a) j -> p h a j", a=2) for b in range(2))
                            tmp = [rope[:, i, :].rearrange("p (h a j) -> p h a j", h=HEADS, a=2) for i in range(4)]
                            v.tensor_tensor(tmp[0], x1, cosb, ALU.mult)
                            v.tensor_tensor(tmp[1], x2, sinb, ALU.mult)
                            v.tensor_tensor(tmp[2], x2, cosb, ALU.mult)
                            chain(v.tensor_tensor(tmp[3], x1, sinb, ALU.mult))
                            v.tensor_tensor(x1, tmp[0], tmp[1], ALU.subtract)
                            v.tensor_tensor(x2, tmp[2], tmp[3], ALU.add).then_inc(roped, 1)
                            dve.drain()
                else:
                    for f in range(12):
                        dve.wait_ge(flip_done, f + 1)
                        v.tensor_tensor(btab[:, f * 512:(f + 1) * 512].rearrange("p (a n) -> p a n", n=GRID_W),
                                        ps[:, 6 + f % 2, :].rearrange("p (a n) -> p a n", n=GRID_W),
                                        cst[:, C_WIN:C_WIN + GRID_W].unsqueeze(1).to_broadcast([P, 8, GRID_W]),
                                        ALU.add).then_inc(flip_used, 1)
                for j in range(PAIRS):
                    dve.wait_ge(qk_ps[l], 2 * j + 2)
                    v.tensor_copy(kT[:, j, :], ps[:, 5 + 2 * (j % 2), :]).then_inc(kT_ev[l], 1)

                def maxima(u):
                    t, j = u // PAIRS, u % PAIRS
                    n = keys[t]
                    sc = ps[:, 2 * (u % 2):2 * (u % 2) + 2, :]
                    dve.wait_ge(sc_done[l], u + 1)
                    if l == 0:
                        chain(v.tensor_reduce(sums[:, u % 2, :], sc[:, :, 0:n], AX, ALU.max))
                        v.tensor_scalar(negm[:, u % 2, :], sums[:, u % 2, :], -SCALE, None, ALU.mult)\
                            .then_inc(negm_rdy[l], 1)
                        return
                    if u:
                        dve.wait_ge(exp_done[l], u)
                    v.tensor_scalar(s_sb[:, :, 0:P], sc[:, :, 0:P], SCALE, None, ALU.mult)
                    if t:
                        m0 = 2 - 2 * (t - 1)
                        bias = btab[:, :].rearrange("p (h n) -> p h n", h=HEADS)[:, 2 * j:2 * j + 2,
                                                                                m0 * GRID_W:(m0 + ROWS) * GRID_W]
                        v.scalar_tensor_tensor(s_sb[:, :, P:n], sc[:, :, P:n], SCALE, bias, ALU.mult, ALU.add)
                    dve.drain()
                    chain(v.tensor_reduce(negm[:, u % 2, :], s_sb[:, :, 0:n], AX, ALU.max))
                    v.tensor_scalar(negm[:, u % 2, :], negm[:, u % 2, :], -1.0, None, ALU.mult).then_inc(negm_rdy[l], 1)

                def combine(u):
                    t, j = u // PAIRS, u % PAIRS
                    n = keys[t]
                    e = prob[u % 2]
                    dve.wait_ge(exp_done[l], u + 1)
                    if l == 1:
                        v.reciprocal(rsum[:, 2 * j:2 * j + 2], sums[:, u % 2, :])
                        dve.drain()
                        if j == PAIRS - 1:
                            dve.wait_ge(pv_done[l], u + 1)
                            v.tensor_tensor(o[:, t, :].rearrange("p (h d) -> p h d", h=HEADS),
                                            tile_ps(3).rearrange("p (h d) -> p h d", h=HEADS),
                                            rsum[:, :].unsqueeze(2).to_broadcast([P, HEADS, HD]), ALU.mult)
                            dve.drain()
                            dve.sem_inc(o_ev[l], 1)
                            dve.sem_inc(o_rdy[l], 1)
                        return
                    chain(v.reciprocal(rsum[:, 0:2], sums[:, u % 2, :]))
                    chain(v.tensor_tensor(rsum[:, 1:2], rsum[:, 1:2], lam[:, 0:1], ALU.mult))
                    chain(v.tensor_scalar(e[:, 1, 0:n], e[:, 1, 0:n], rsum[:, 1:2], None, ALU.mult))
                    v.scalar_tensor_tensor(e[:, 0, 0:n], e[:, 0, 0:n], rsum[:, 0:1], e[:, 1, 0:n],
                                           ALU.mult, ALU.subtract).then_inc(comb_done[l], 1)
                    dve.drain()

                def head_norm(t):
                    dve.wait_ge(o_ev[l], t + 1)
                    ov = o[:, t, :].rearrange("p (h d) -> p h d", d=P)
                    chain(v.tensor_tensor(t1[:, :], o[:, t, :], o[:, t, :], ALU.mult))
                    chain(v.tensor_reduce(var[:, :], t1[:, :].rearrange("p (h d) -> p h d", d=P), AX, ALU.add))
                    chain(v.tensor_scalar(var[:, :], var[:, :], 1.0 / P, EPS, ALU.mult, ALU.add))
                    rsqrt(rstd[:, :], var[:, :], newt[:, :])
                    chain(v.tensor_tensor(ov, ov, rstd[:, :].unsqueeze(2).to_broadcast([P, 8, P]), ALU.mult))
                    v.tensor_tensor(ov, ov, subg[:, :].unsqueeze(1).to_broadcast([P, 8, P]), ALU.mult)\
                        .then_inc(o_rdy[l], 1)
                    dve.drain()

                if l == 1:
                    dve.drain()
                for u in range(UNITS):
                    maxima(u)
                    if u:
                        combine(u - 1)
                    if l == 0 and u % PAIRS == 2 and u > PAIRS:
                        head_norm(u // PAIRS - 1)
                combine(UNITS - 1)
                if l == 0:
                    head_norm(NT - 1)
                dve.wait_ge(st_free, RING + WO0[l] + RING)
                layer_norm(l, 0, tile_ps)
                modulate(l, 1, xm_rdy[l])

                def col(a, n):
                    return rt[:, a:a + n]

                lg = col(128, NT * 36).rearrange("p (t n) -> p t n", t=NT)
                gl, el = lg[:, :, 0:NG], lg[:, :, NG:]
                rx = col(64, 15).rearrange("p (t n) -> p t n", t=NT)
                iota = cst[:, C_IOTA:C_IOTA + P]

                def b3(a, n):
                    return a.unsqueeze(2).to_broadcast([P, NT, n])

                def iota3(n):
                    return iota[:, 0:n].unsqueeze(1).to_broadcast([P, NT, n])

                def first_max(vals, n, mx, one):
                    tmp = col(288, NT * n).rearrange("p (t n) -> p t n", t=NT)
                    chain(v.tensor_reduce(mx, vals, AX, ALU.max))
                    chain(v.tensor_tensor(tmp, vals, b3(mx, n), ALU.is_equal))
                    chain(v.tensor_scalar(tmp, tmp, -1000.0, 1000.0, ALU.mult, ALU.add))
                    chain(v.tensor_tensor(tmp, tmp, iota3(n), ALU.add))
                    chain(v.tensor_reduce(col(20, NT), tmp, AX, ALU.min))
                    chain(v.tensor_tensor(one, iota3(n), b3(col(20, NT), n), ALU.is_equal))

                a_all = col(384, 96).rearrange("p (t e) -> p t e", t=NT)
                e1 = col(480, 96).rearrange("p (t e) -> p t e", t=NT)
                e2 = col(1024, 96).rearrange("p (t e) -> p t e", t=NT)
                dve.wait_ge(rt_pe[l], 1)
                chain(v.tensor_tensor(lg, ps[:, 6, 0:NT * 36].rearrange("p (t n) -> p t n", t=NT),
                                      br[:, l, :].unsqueeze(1).to_broadcast([P, NT, 36]), ALU.add))
                oneg = col(32, NT * NG).rearrange("p (t n) -> p t n", t=NT)
                first_max(gl, NG, col(0, NT), oneg)
                v.tensor_tensor(rx[:, :, 0:NG], gl, b3(col(0, NT), NG), ALU.subtract)
                pen = col(48, NT * NG).rearrange("p (t n) -> p t n", t=NT)
                chain(v.tensor_scalar(pen, oneg, BIG, -BIG, ALU.mult, ALU.add))
                e4 = el.rearrange("p t (g n) -> p t g n", g=NG)
                for t in range(NT):
                    chain(v.tensor_tensor(e4[:, t], e4[:, t], oneg[:, t, :].unsqueeze(2).to_broadcast([P, NG, EPG]), ALU.mult))
                    chain(v.tensor_tensor(e4[:, t], e4[:, t], pen[:, t, :].unsqueeze(2).to_broadcast([P, NG, EPG]), ALU.add))
                first_max(el, NE, col(3, NT), e1)
                chain(v.scalar_tensor_tensor(el, e1, -2 * BIG, el, ALU.mult, ALU.add))
                first_max(el, NE, col(6, NT), e2)
                v.tensor_tensor(rx[:, :, NG], col(6, NT), col(3, NT), ALU.subtract).then_inc(rt_dve[l], 1)
                v.tensor_tensor(a_all, e1, e2, ALU.add).then_inc(rt_dve[l], 1)
                dve.wait_ge(rt_pe[l], 2)
                cnt = rt[0:NE, 590:591]
                chain(v.tensor_copy(cnt, ps[0:NE, 5, 0:1]))
                chain(v.tensor_scalar(rt[0:NE, 592:598], cst[0:NE, C_THR:C_THR + 6], cnt, None, ALU.is_lt))
                chain(v.tensor_reduce(rt[0:NE, 600:601], rt[0:NE, 592:598], AX, ALU.add))
                v.tensor_copy(rt[0:NE, 601:602], rt[0:NE, 592:593])
                v.tensor_scalar(rt[0:NE, 640:768], cst[0:NE, C_ONE:C_ONE + P], rt[0:NE, 600:601], None, ALU.mult)
                dve.drain()
                dve.sem_inc(rt_dve[l], 1)
                dve.wait_ge(rt_pe[l], 3)
                first_b, ordn, last_b = rt[0:NE, 604:605], rt[0:NE, 605:606], rt[0:NE, 606:607]
                chain(v.tensor_copy(rt[0:NE, 604:606], ps[0:NE, 4, 0:2]))
                v.tensor_tensor(last_b, first_b, rt[0:NE, 600:601], ALU.add)
                used = rt[0:NE, 601:602]
                v.tensor_scalar(rt[0:NE, 800:832], iota[0:NE, 0:NE], ordn, used, ALU.is_equal, ALU.mult)
                v.tensor_scalar(rt[0:NE, 880:928], iota[0:NE, 0:48], first_b, used, ALU.is_equal, ALU.mult)
                chain(v.tensor_scalar(rt[0:NE, 832:880], iota[0:NE, 0:48], first_b, None, ALU.is_ge))
                v.scalar_tensor_tensor(rt[0:NE, 832:880], iota[0:NE, 0:48], last_b, rt[0:NE, 832:880],
                                       ALU.is_lt, ALU.mult)
                dve.drain()
                dve.sem_inc(rt_dve[l], 1)
                sp_ = col(928, 96).rearrange("p (t e) -> p t e", t=NT)
                chain(v.tensor_copy(sp_, ps[:, 7, 0:96].rearrange("p (t e) -> p t e", t=NT)))
                chain(v.tensor_scalar(col(768, NE), ps[:, 3, 0:NE], float(BLK), None, ALU.mult))
                chain(v.tensor_tensor(sp_, sp_, col(768, NE).unsqueeze(1).to_broadcast([P, NT, NE]), ALU.add))
                for k, one in enumerate((e1, e2)):
                    chain(v.tensor_tensor(one, one, sp_, ALU.mult))
                    chain(v.tensor_reduce(col(1184, 2 * NT).rearrange("p (t k) -> p t k", k=2)[:, :, k], one, AX, ALU.add))
                chain(v.tensor_copy(sloti[:, :], col(1184, 2 * NT)))
                si = rt[:, 2000:2000 + 12].bitcast(I32)
                v.tensor_single_scalar(si[:, 0:6], sloti[:, :], 6, op=ALU.arith_shift_right)
                chain(v.tensor_single_scalar(si[:, 6:12], sloti[:, :], BLK - 1, op=ALU.bitwise_and))
                sf = col(2016, 12)
                chain(v.tensor_copy(sf, si))
                rowf = col(2032, 2 * NT)
                for k in range(TOPK):
                    v.tensor_scalar(rowf.rearrange("p (t k) -> p t k", k=TOPK)[:, :, k], cst[:, C_TOK:C_TOK + NT],
                                    1.0 + k * NT * P, None, ALU.add)
                dve.drain()
                for i in range(2 * NT):
                    v.tensor_scalar(col(1200 + i * BLK, BLK), iota[:, 0:BLK], sf[:, 6 + i:7 + i], None, ALU.is_equal)
                    v.tensor_scalar(col(1600 + i * NBX, NBX), iota[:, 0:NBX], sf[:, i:i + 1],
                                    rowf[:, i:i + 1], ALU.is_equal, ALU.mult)
                dve.drain()
                dve.sem_inc(rt_dve[l], 1)
                dve.wait_ge(rt_pe[l], 4)
                chain(v.tensor_scalar(tabi[:, T_LAST:T_N], ps[0:1, 2, T_NBLK:T_NBLK + 1], -1.0, None, ALU.add))
                v.tensor_copy(tabi[:, 0:T_LAST], ps[0:1, 2, 0:T_LAST]).then_inc(tab_rdy[l], 1)
                dve.wait_ge(rt_pe[l], 5)
                val, empty, half = (rt[0:BLK, 2048 + i * NBX:2048 + (i + 1) * NBX] for i in range(3))
                chain(v.tensor_scalar(val, ps[0:BLK, 1, 0:NBX], -1.0, None, ALU.add))
                chain(v.tensor_scalar(empty, val, 0.0, None, ALU.is_lt))
                chain(v.tensor_scalar(half, cst[0:BLK, C_TOK:C_TOK + 1].to_broadcast([BLK, NBX]),
                                      float(TOPK * NT * P + 1), None, ALU.add))
                chain(v.tensor_tensor(half, half, empty, ALU.mult))
                chain(v.tensor_tensor(rowi[:, :], val, half, ALU.add))
                chain(v.tensor_scalar(half, val, float(NT * P), float(NT * P), ALU.is_ge, ALU.mult))
                chain(v.tensor_tensor(val, val, half, ALU.subtract))
                v.tensor_scalar(toki[:, :], val, 0.0, None, ALU.max).then_inc(tok_rdy[l], 1)
                dve.wait_ge(rt_act[l], 1)
                chain(v.tensor_reduce(col(9, NT), rx[:, :, 0:NG], AX, ALU.add))
                chain(v.tensor_scalar(col(12, NT), rx[:, :, NG], 1.0, None, ALU.add))
                chain(v.tensor_tensor(col(9, NT), col(9, NT), col(12, NT), ALU.mult))
                chain(v.reciprocal(gatew[:, 0, :], col(9, NT)))
                chain(v.tensor_tensor(gatew[:, 1, :], gatew[:, 0, :], rx[:, :, NG], ALU.mult))

                dve.wait_ge(tab_rdy[l], 1)
                last_blk = table(dve, T_LAST, 11, NB - 1)

                def split_rest(b, ordn, chunks):
                    rests(dve, v, l, b, ordn, [s for s in chunks if s not in POOL_CHUNKS])

                def x_rest(b):
                    dve.wait_ge(xsh_rdy[l], b + 1)
                    v.tensor_tensor(xs[:, :, BLK:2 * BLK], ps[:, 0, :].rearrange("p (k n) -> p k n", k=KD),
                                    xs[:, :, 0:BLK].bitcast(F32), ALU.subtract).then_inc(xsl_rdy[l], 1)

                def y_sum(b):
                    dve.wait_ge(*chunk_use(l, RING - 1, b + 1))
                    chain(v.tensor_copy(yl[:, :], ps_t[BLK:P, 5 * 512:7 * 512]))
                    if not (isinstance(b, int) and b == 0):
                        dve.wait_ge(y_wr[l], b * 16)
                    v.tensor_tensor(yo[:, :], ps_t[0:BLK, 5 * 512:7 * 512], yl[:, :], ALU.add).then_inc(yo_rdy[l], 1)

                def hidden(b):
                    dve.wait_ge(sg_rdy[l], b + 1)
                    dve.wait_ge(gut_done[l], b * 2 + 2)
                    if not (isinstance(b, int) and b == 0):
                        dve.wait_ge(hh_rdy[l], b)
                        dve.wait_ge(hl_rdy[l], b)
                    v.tensor_tensor(hm[:, :], sg[:, :], ps[:, 4, 0:4 * BLK], ALU.mult).then_inc(hm_rdy[l], 1)
                    dve.wait_ge(hh_rdy[l], b + 1)
                    v.tensor_tensor(hs[:, :, BLK:2 * BLK], hm[:, :].rearrange("p (k n) -> p k n", k=4),
                                    hs[:, :, 0:BLK].bitcast(F32), ALU.subtract).then_inc(hl_rdy[l], 1)

                def body(b, before=None):
                    ord_next = table(dve, T_ORD + 1 + b, 0, NE - 1)
                    first_next = table(dve, T_FIRST + 1 + b, 0, 1)
                    with dve.If(first_next > 0):
                        split_rest(b + 1, ord_next, range(2))
                    if before is not None:
                        ordn = table(dve, T_ORD + b, 0, NE - 1)
                        first = table(dve, T_FIRST + b, 0, 1)
                        with dve.If(first > 0):
                            split_rest(b, ordn, range(GU, RING))
                    else:
                        split_rest(b, 0, range(GU, RING))
                    x_rest(b + 1)
                    hidden(b)
                    if before is not None:
                        y_sum(before)
                    with dve.If(first_next > 0):
                        split_rest(b + 1, ord_next, range(2, GU))

                split_rest(0, 0, range(GU))
                x_rest(0)
                body(0)
                body(1, 0)
                with dve.Fori(1, last_blk) as b:
                    body(b + 1, b)
                y_sum(last_blk)
                dve.wait_ge(yg_ld[l], 16)
                for t in range(NT):
                    chain(v.tensor_scalar(o[:, t, :], ypair[:, t, :], gatew[:, 0, t:t + 1], None, ALU.mult))
                    chain(v.scalar_tensor_tensor(o[:, t, :], ypair[:, NT + t, :], gatew[:, 1, t:t + 1], o[:, t, :],
                                                 ALU.mult, ALU.add))
                layer_norm(l, 1, lambda t: o[:, t, :])


_INS = ['x_prompt', 'x_sample', 'cache_a_k', 'cache_a_v', 'cache_b_k', 'cache_b_v', 'c', 'c_ctx', 'w_ada', 'b_ada',
        'ln_g', 'ln_b', 'w_qkv_a', 'lam_a', 'subln_a', 'w_o_a', 'w_qkv_b', 'rpb_b', 'w_o_b', 'w_rg', 'b_rg', 'w_re',
        'b_re', 'w_gate', 'w_up', 'w_down']
_OUTS = [(1, 128, 1024), (1, 256, 1024), (1, 1, 128, 16, 64), (1, 1, 128, 8, 128), (1, 1, 128, 16, 64),
         (1, 1, 128, 16, 64)]


def kernel(**inputs):
    import numpy as _np
    import concourse.bacc as _bacc
    from concourse import mybir as _mybir
    from concourse.bass_utils import run_bass_kernel_spmd as _run

    nc = _bacc.Bacc("TRN2", target_bir_lowering=False, num_devices=1)
    arrays, args = {}, []
    for name in _INS:
        a = _np.ascontiguousarray(inputs[name])
        arrays[f"in_{name}_dram"] = a
        args.append(nc.dram_tensor(f"in_{name}_dram", a.shape, _mybir.dt.from_np(a.dtype), kind="ExternalInput").ap())
    a = constants()
    arrays["in_consts_dram"] = a
    args.append(nc.dram_tensor("in_consts_dram", a.shape, _mybir.dt.from_np(a.dtype), kind="ExternalInput").ap())
    for i, shape in enumerate(_OUTS):
        args.append(nc.dram_tensor(f"out_{i}_dram", shape, _mybir.dt.float32, kind="ExternalOutput").ap())
    backbone_kernel(nc, *args)
    r = _run(nc, [arrays], core_ids=[0])
    return tuple(r.results[0][f"out_{i}_dram"] for i in range(len(_OUTS)))
```

```python
from contextlib import ExitStack
import math

import numpy as np
import concourse.bass as bass
from concourse import mybir

P = 128
D = 1024
KD = D // P
NT = 3
LAYERS = 2
HEADS = 16
HD = 64
PAIRS = HEADS // 2
NE = 32
NG = 4
EPG = NE // NG
DE = 512
TOPK = 2
BLK = 64
NB = (NT * P * TOPK + NE * (BLK - 1)) // BLK
NBX = NB + 2
RING = 6
GU, DN = 4, 2
POOL_CHUNKS = (3, 5)
CH = 2048
GRID_W = 64
NA_KH, NA_KW = 8, 16
ROWS = 256 // GRID_W
BM = 6
SCALE = HD ** -0.5
ALPHA = (2.0 * LAYERS) ** 0.25
EPS = 1e-5
LAM_INIT = 0.8 - 0.6 * math.exp(0.0)
WO_K = (2, 2, 1, 1, 1, 1)
BIG = 1e30

F32 = mybir.dt.float32
F32R = mybir.dt.float32r
I32 = mybir.dt.int32
ACT = mybir.ActivationFunctionType
ALU = mybir.AluOpType
AX = mybir.AxisListType.X

C_ID, C_II, C_FLIP, C_TRI, C_ONE, C_IOTA, C_TOK, C_ROPE, C_WIN, C_ZERO, C_THR = np.cumsum(
    [0, P, BLK, P, P, P, P, NT, 2 * 2 * 32, GRID_W, P]).tolist()
C_N = C_THR + 8
T_LIST, T_ORD, T_FIRST, T_NACT, T_NBLK = 0, 32, 32 + 48, 32 + 96, 32 + 97
T_LAST = T_NBLK + 1
T_N = T_LAST + 1


def constants():
    c = np.zeros((P, C_N), np.float32)
    p = np.arange(P)
    c[p, C_ID + p] = 1.0
    c[p, C_II + p % BLK] = 1.0
    c[p, C_FLIP + (p // 64) * 64 + 63 - p % 64] = 1.0
    c[:, C_TRI:C_TRI + P] = p[:, None] < p[None, :]
    c[:, C_ONE:C_ONE + P] = 1.0
    c[:, C_IOTA:C_IOTA + P] = p[None, :]
    c[:, C_TOK:C_TOK + NT] = p[:, None] + P * np.arange(NT)[None, :]
    t = np.arange(256)
    pos = np.stack([t // GRID_W, t % GRID_W], -1).astype(np.float32)
    quarter = HD // 4
    inv = (np.float32(10000.0) ** (-np.arange(quarter, dtype=np.float32) / np.float32(quarter))).astype(np.float32)
    ang = (pos[:, :, None] * inv).reshape(2, P, 32)
    for i in range(2):
        c[:, C_ROPE + i * 64:C_ROPE + i * 64 + 32] = np.cos(ang[i])
        c[:, C_ROPE + i * 64 + 32:C_ROPE + i * 64 + 64] = np.sin(ang[i])
    q, k = p[:, None] % 64, np.arange(GRID_W)[None, :]
    start = np.clip(q - NA_KW // 2, 0, GRID_W - NA_KW)
    c[:, C_WIN:C_WIN + GRID_W] = np.where((k >= start) & (k < start + NA_KW), 0.0, -BIG)
    c[:, C_THR:C_THR + 6] = BLK * np.arange(6)[None, :]
    return c


def backbone_kernel(nc, x_prompt, x_sample, cache_a_k, cache_a_v, cache_b_k, cache_b_v, c, c_ctx,
                    w_ada, b_ada, ln_g, ln_b, w_qkv_a, lam_a, subln_a, w_o_a, w_qkv_b, rpb_b, w_o_b,
                    w_rg, b_rg, w_re, b_re, w_gate, w_up, w_down, consts,
                    y_prompt, y_sample, new_a_k, new_a_v, new_b_k, new_b_v):
    ctx = ExitStack()
    with ctx:
        def sb(name, shape, dt=F32):
            return ctx.enter_context(nc.sbuf_tensor(name, shape, dt))

        def overlay(tensors):
            with ExitStack() as s:
                return [s.enter_context(nc.sbuf_tensor(n, shape, dt)) for n, shape, dt in tensors]

        def sem(name):
            return ctx.enter_context(nc.semaphore(name))

        def sem2(name):
            return [sem(f"{name}_{l}") for l in range(LAYERS)]

        cst = sb("cst", [P, C_N])
        x = sb("x", [P, NT, D])
        raw = sb("raw", [P, RING, CH])
        modb = sb("modb", [P, 4, D])
        wr = sb("wr", [P, LAYERS, KD, NG + NE])
        br = sb("br", [P, LAYERS, NG + NE])
        condr = sb("condr", [P, 2, KD])
        cond = sb("cond", [P, KD, 2])
        lamb = sb("lamb", [P, 4 * HD])
        lam = sb("lam", [P, 4])
        subg = sb("subg", [P, P])
        negm = sb("negm", [P, 2, 2])
        sums = sb("sums", [P, 2, 2])
        rsum = sb("rsum", [P, 2 * HEADS])
        st = sb("st", [P, 2, 6])
        mv = sb("mv", [P, NT, 2])
        var = sb("var", [P, 8])
        newt = sb("newt", [P, 8])
        rstd = sb("rstd", [P, 8])
        mbias = sb("mbias", [1, 512])
        gatew = sb("gatew", [P, 2, NT])
        sloti = sb("sloti", [P, 2 * NT], I32)
        rowi = sb("rowi", [BLK, NBX], I32)
        idy = sb("idy", [BLK, 1], I32)
        toki = sb("toki", [BLK, NBX], I32)
        idx = sb("idx", [BLK, 1], I32)
        tabi = sb("tabi", [1, T_N], I32)

        mrow, badb = overlay([("mrow", [2, 6 * D], F32), ("badb", [2, 6 * D], F32)])
        qkv, hT, qT, kT, kctx, vctx, o = overlay([
            ("qkv", [P, NT, 3 * D], F32), ("hT", [P, KD, NT * P], F32), ("qT", [P, KD, NT * P], F32),
            ("kT", [P, KD, 4 * P], F32), ("kctx", [P, D], F32), ("vctx", [P, D], F32), ("o", [P, NT, D], F32)])
        wh, wl = overlay([("wh", [P, RING, CH], F32R), ("wl", [P, RING, CH], F32R)])
        sb("large_region", [P, 2 * RING * CH])
        rope, t1 = overlay([("rope", [P, 4, 512], F32), ("t1", [P, D], F32)])
        (mst,) = overlay([("mst", [2, 3, 512], F32)])
        (btab,) = overlay([("btab", [P, HEADS * BM * GRID_W], F32)])
        xs, hs, xg, gsb, usb, sg, hm, yl, yo = overlay([
            ("xs", [P, KD, 2 * BLK], F32R), ("hs", [P, 4, 2 * BLK], F32R), ("xg", [BLK, D], F32),
            ("gsb", [P, DE], F32), ("usb", [P, DE], F32), ("sg", [P, 4 * BLK], F32), ("hm", [P, 4 * BLK], F32),
            ("yl", [BLK, D], F32), ("yo", [BLK, D], F32)])
        sb("small_region", [P, 6144])

        hTf = hT[:, :, :].rearrange("p k n -> p (k n)")
        s_sb = hTf[:, 0:768].rearrange("p (h n) -> p h n", h=2)
        prob = [hTf[:, 768 * (1 + i):768 * (2 + i)].rearrange("p (h n) -> p h n", h=2) for i in range(2)]
        probT = hTf[:, 2304:3072].rearrange("p (h n) -> p h n", h=2)
        oT = qT
        lnb = kT[:, :, :].rearrange("p k n -> p (k n)").rearrange("p (v d) -> p v d", v=4)
        rt = kT[:, :, :].rearrange("p k n -> p (k n)")
        ypair = qkv[:, :, :].rearrange("p t n -> p (t n)").rearrange("p (s d) -> p s d", d=D)
        hank = o[:, :, :].rearrange("p t n -> p (t n)")

        ps_t = ctx.enter_context(nc.psum_tensor("ps", [P, 8 * 512], F32))
        ps = ps_t[:, :].rearrange("p (b n) -> p b n", b=8)

        def tile_ps(t):
            return ps_t[:, 1024 * t:1024 * (t + 1)]

        ident = cst[:, C_ID:C_ID + P]
        ident64 = cst[0:BLK, C_ID:C_ID + BLK]
        stack2 = cst[:, C_II:C_II + BLK]
        ones = cst[:, C_ONE:C_ONE + P]
        tri = cst[:, C_TRI:C_TRI + P]

        mdram = nc.dram_tensor("mdram", (LAYERS, 2, 6 * D), F32).ap()
        xmod = nc.dram_tensor("xmod", (NT * P, D), F32).ap()
        ybuf = nc.dram_tensor("ybuf", (TOPK * NT * P + BLK, D), F32).ap()
        bpad = nc.dram_tensor("bpad", (2, HEADS * BM, P), F32).ap()

        ld_small = sem("ld_small")
        ld_bada = sem("ld_bada")
        st_land = [sem(f"st_land{i}") for i in range(RING)]
        st_free = sem("st_free")
        cond_rdy = sem("cond_rdy")
        ada_evac = sem("ada_evac")
        mrow_saved = sem("mrow_saved")
        mbias_ld = sem("mbias_ld")
        mblk_saved = [sem(f"mblk_saved{i}") for i in range(3)]
        mblk_ev = sem("mblk_ev")
        mod_ld, mod_used, lnb_ld = sem("mod_ld"), sem("mod_used"), sem("lnb_ld")
        lam_rdy = sem("lam_rdy")
        pad_zero, pad_done = sem("pad_zero"), sem("pad_done")
        hank_ld, flip_done, flip_used = sem("hank_ld"), sem("flip_done"), sem("flip_used")
        out_done = sem("out_done")
        ctx_ld = sem2("ctx_ld")
        h_rdy, hT_ps, hT_rdy = sem2("h_rdy"), sem2("hT_ps"), sem2("hT_rdy")
        qkv_done, qkv_ev = sem2("qkv_done"), sem2("qkv_ev")
        roped = sem("roped")
        qk_ps, qT_ev, kT_ev = sem2("qk_ps"), sem2("qT_ev"), sem2("kT_ev")
        sc_done, negm_rdy, exp_done, comb_done = sem2("sc_done"), sem2("negm_rdy"), sem2("exp_done"), sem2("comb_done")
        pT_done, pT_ev, pv_done, o_ev, o_rdy = sem2("pT_done"), sem2("pT_ev"), sem2("pv_done"), sem2("o_ev"), sem2("o_rdy")
        oT_ps, oT_rdy = sem2("oT_ps"), sem2("oT_rdy")
        xm_rdy, xmod_w, xT_ps, xT_rdy = sem2("xm_rdy"), sem2("xmod_w"), sem2("xT_ps"), sem2("xT_rdy")
        rt_pe, rt_dve, rt_act = sem2("rt_pe"), sem2("rt_dve"), sem2("rt_act")
        tab_rdy, tok_rdy = sem2("tab_rdy"), sem2("tok_rdy")
        moe_land = [[sem(f"moe_land{l}_{i}") for i in range(RING)] for l in range(LAYERS)]
        gu_high, gu_used, dn_high, dn_used = sem2("gu_high"), sem2("gu_used"), sem2("dn_high"), sem2("dn_used")
        gu_rest, up_rest, dn_rest, dn2_rest = sem2("gu_rest"), sem2("up_rest"), sem2("dn_rest"), sem2("dn2_rest")
        idx_rdy, idy_rdy, gath, xg_used = sem2("idx_rdy"), sem2("idy_rdy"), sem2("gath"), sem2("xg_used")
        xsh_rdy, xsl_rdy = sem2("xsh_rdy"), sem2("xsl_rdy")
        g_rdy, u_rdy, gut_done, sg_rdy, hm_rdy = sem2("g_rdy"), sem2("u_rdy"), sem2("gut_done"), sem2("sg_rdy"), sem2("hm_rdy")
        hh_rdy, hl_rdy, yo_rdy, y_wr = sem2("hh_rdy"), sem2("hl_rdy"), sem2("yo_rdy"), sem2("y_wr")
        pool_steps, pe_steps = sem("pool_steps"), sem("pe_steps")
        yg_ld, x_rdy = sem2("yg_ld"), sem2("x_rdy")

        ADA = 24
        QKV0 = [ADA, 2 * ADA + 18]
        WO0 = [q + 12 for q in QKV0]
        ADA1 = [WO0[0] + RING, WO0[0] + RING + ADA // 2]
        MOE0 = [ADA1[1], WO0[1] + RING]
        w_qkv, w_o = [w_qkv_a, w_qkv_b], [w_o_a, w_o_b]
        keys = [P, 3 * P, 3 * P]
        key0 = [0, P, P]
        UNITS = NT * PAIRS

        def ada_end(b):
            return RING + ADA1[b // 6] + 2 * (b % 6) + 2

        ADA_BANK = (6, 7, 6, 7, 0, 7) + (7, 4) * 3

        def wait_chunk(eng, n):
            eng.wait_ge(st_land[n % RING], 16 * (n // RING + 1))

        def table(eng, col, lo, hi):
            return eng.value_load(tabi[0:1, bass.ds(col, 1)] if not isinstance(col, int) else tabi[0:1, col:col + 1],
                                  min_val=lo, max_val=hi)

        def wait_apart(eng, step, s, value):
            eng.wait_ge(s, value)
            eng.sem_inc(step, 1)

        def high(l, s, e):
            return (gu_high[l], e * GU + s + 1) if s < GU else (dn_high[l], e * DN + (s - GU + 1))

        def rest(l, s, e):
            if s < 3:
                return gu_rest[l], e * 3 + (s + 4)
            return (up_rest, dn_rest, dn2_rest)[s - 3][l], e + 2

        def chunk_use(l, s, b):
            return (gu_used[l], b * GU + (s + 1 - GU)) if s < GU else (dn_used[l], b * DN + (s + 1 - GU - DN))

        def rests(eng, unit, l, b, ordn, chunks):
            for s in chunks:
                eng.wait_ge(*high(l, s, ordn))
                if not (isinstance(b, int) and b == 0):
                    eng.wait_ge(*chunk_use(l, s, b))
                unit.tensor_tensor(wl[:, s, :], raw[:, s, :], wh[:, s, :].bitcast(F32), ALU.subtract)\
                    .then_inc((gu_rest, gu_rest, gu_rest, up_rest, dn_rest, dn2_rest)[s][l], 1)

        block = ctx.enter_context(nc.Block())

        @block.sync
        def _(sp):
            def taken(l, s, i):
                if s < 3:
                    return gu_rest[l], i * 3 + (s + 1)
                return (up_rest, dn_rest, dn2_rest)[s - 3][l], i + 1

            with sp.Fori(0, 4) as m:
                for s in range(RING):
                    col = m * 1536 + (s // 2) * 512
                    sp.wait_ge(st_free, m * RING + s + 1)
                    sp.dma_start(
                        raw[:, s, :].rearrange("p (k n) -> p k n", k=4),
                        w_ada[0, :, bass.ds(col, 512)].rearrange("(p k) n -> p k n", k=KD)
                        [:, 4 * (s % 2):4 * (s % 2) + 4, :]).then_inc(st_land[s], 16)

            def load_bias(b):
                if b:
                    sp.wait_ge(st_free, ada_end(b - 1))
                sp.dma_start(mbias[:, :], b_ada[1:2, b * 512:(b + 1) * 512]).then_inc(mbias_ld, 16)

            def load_ada(half):
                for i in range(6):
                    b = 6 * half + i
                    for c in range(2):
                        n = ADA1[half] + 2 * i + c
                        s = n % RING
                        if half and i < 3:
                            sp.wait_ge(*taken(0, s, n_act))
                        else:
                            sp.wait_ge(st_free, n + 1)
                        sp.dma_start(
                            raw[:, s, :].rearrange("p (k n) -> p k n", k=4),
                            w_ada[1, :, b * 512:(b + 1) * 512].rearrange("(p k) n -> p k n", k=KD)
                            [:, 4 * c:4 * c + 4, :]).then_inc(st_land[s], 16)
                    if i >= 2:
                        load_bias(b - 2)
                load_bias(6 * half + 4)
                load_bias(6 * half + 5)

            for l in range(LAYERS):
                wq = w_qkv[l].rearrange("a (p k) n -> p (a k) n", k=KD)
                for cidx in range(12):
                    n = QKV0[l] + cidx
                    g, ck = cidx // 4, cidx % 4
                    sp.wait_ge(st_free, n + 1)
                    sp.dma_start(raw[:, n % RING, :].rearrange("p (k n) -> p k n", k=2),
                                 wq[:, 2 * ck:2 * ck + 2, g * D:(g + 1) * D]).then_inc(st_land[n % RING], 16)
                wo = w_o[l].rearrange("a (p k) n -> p (a k) n", k=KD)
                k = 0
                for cidx, nk in enumerate(WO_K):
                    n = WO0[l] + cidx
                    sp.wait_ge(st_free, n + 1)
                    sp.dma_start(raw[:, n % RING, 0:nk * D].rearrange("p (k n) -> p k n", k=nk),
                                 wo[:, k:k + nk, :]).then_inc(st_land[n % RING], 16)
                    k += nk

                if l == 0:
                    load_ada(0)
                sp.wait_ge(tab_rdy[l], 1)
                n_act = table(sp, T_NACT, 2, NE)

                def load(i, chunks):
                    e = table(sp, T_LIST + i, 0, NE - 1)
                    for s in chunks:
                        if s >= GU or isinstance(i, int):
                            sp.wait_ge(st_free, MOE0[l] + s + 1)
                        if not isinstance(i, int):
                            sp.wait_ge(*taken(l, s, i))
                        w = (w_gate, w_up, w_down)[s // 2]
                        src = w[l, bass.ds(e, 1)]
                        kk = KD if s < GU else 4
                        part = kk // 2
                        src = src.rearrange("a (p k) n -> p (a k) n", k=kk)[:, part * (s % 2):part * (s % 2 + 1), :]
                        sp.dma_start(raw[:, s, :].rearrange("p (k n) -> p k n", k=part), src).then_inc(moe_land[l][s], 16)

                load(0, range(GU))
                with sp.Fori(1, n_act) as i:
                    load(i, range(2))
                    load(i - 1, range(GU, RING))
                    load(i, range(2, GU))
                load(n_act - 1, range(GU, RING))
                if l == 0:
                    load_ada(1)

        @block.gpsimd
        def _(pool):
            for hf in range(2):
                pool.dma_start(bpad[hf], consts[0:HEADS * BM, C_ZERO:C_ZERO + P]).then_inc(pad_zero, 16)
            pool.wait_ge(pad_zero, 32)
            for hf in range(2):
                pool.dma_start(bpad[hf].rearrange("(h m) n -> h m n", m=BM)[:, :, 48:48 + 2 * NA_KW - 1],
                               rpb_b[0, :, 5 - hf:5 - hf + BM, :]).then_inc(pad_done, 16)

            def rows(l, cnd, vec):
                return mdram[l, cnd:cnd + 1, vec * D:(vec + 1) * D].to_broadcast([P, D])

            def load_mod(l, stage):
                for cnd in range(2):
                    for i, vec in enumerate((3 * stage + 1, 3 * stage)):
                        pool.dma_start(modb[:, 2 * cnd + i, :], rows(l, cnd, vec)).then_inc(mod_ld, 16)

            def load_ln(l, stage):
                for cnd in range(2):
                    pool.dma_start(lnb[:, cnd, :], rows(l, cnd, 3 * stage + 2)).then_inc(lnb_ld, 16)
                for i, w in enumerate((ln_g, ln_b)):
                    pool.dma_start(lnb[:, 2 + i, :], w[l, stage:stage + 1, :].to_broadcast([P, D])).then_inc(lnb_ld, 16)

            pool.wait_ge(ada_evac, 3 + 12)
            pool.dma_start(mdram[0], mrow[:, :]).then_inc(mrow_saved, 16)
            pool.wait_ge(mrow_saved, 16)
            load_mod(0, 0)

            for l in range(LAYERS):
                ck, cv = ((cache_a_k, cache_a_v), (cache_b_k, cache_b_v))[l]
                pool.dma_start(kctx[:, :], ck[0, 0].rearrange("t h d -> t (h d)")).then_inc(ctx_ld[l], 16)
                pool.dma_start(vctx[:, :], cv[0, 0].rearrange("t h d -> t (h d)")).then_inc(ctx_ld[l], 16)
                if l == 1:
                    for r in range(2):
                        if r:
                            pool.wait_ge(flip_done, 6)
                        for hf in range(2):
                            src = bass.AP(tensor=bpad.tensor, offset=(hf * HEADS * BM + r * 8 * BM) * P,
                                          ap=[[1, 64], [P, 8 * BM], [1, GRID_W]])
                            if r == 0 and hf == 0:
                                pool.wait_ge(pad_done, 32)
                                pool.wait_ge(x_rdy[0], NT)
                            pool.dma_start(hank[64 * hf:64 * hf + 64, :].rearrange("p (a n) -> p a n", n=GRID_W),
                                           src).then_inc(hank_ld, 16)
                nk, nv = ((new_a_k, new_a_v), (new_b_k, new_b_v))[l]
                pool.wait_ge(qkv_ev[l], 6)
                pool.dma_start(nk[0, 0].rearrange("t h d -> t (h d)"), qkv[:, 0, D:2 * D]).then_inc(out_done, 16)
                pool.wait_ge(qkv_ev[l], 9)
                pool.dma_start(nv[0, 0].rearrange("t h d -> t (h d)"), qkv[:, 0, 2 * D:3 * D]).then_inc(out_done, 16)
                pool.wait_ge(mod_used, 2 * l + 1)
                if l == 1:
                    for i in range(3):
                        pool.wait_ge(mblk_saved[i], 64)
                load_mod(l, 1)
                pool.wait_ge(pv_done[l], UNITS)
                load_ln(l, 0)
                pool.wait_ge(xm_rdy[l], NT)
                pool.dma_start(xmod.rearrange("(t p) d -> p t d", p=P), qkv[:, :, 0:D]).then_inc(xmod_w[l], 16)

                pool.wait_ge(tok_rdy[l], 1)
                pool.wait_ge(tab_rdy[l], 1)
                n_blk = table(pool, T_NBLK, 12, NB)
                pool.wait_ge(xmod_w[l], 16)
                pool.wait_ge(out_done, 32 * (l + 1))

                def gather(b):
                    pool.tensor_copy(idx[:, :], toki[:, bass.ds(b, 1)] if not isinstance(b, int) else toki[:, b:b + 1])\
                        .then_inc(idx_rdy[l], 1)
                    wait_apart(pool, pool_steps, idx_rdy[l], b + 1)
                    pool.indirect_dma_start(out=xg[:, :], out_offset=None, in_=xmod,
                                            in_offset=bass.IndirectOffsetOnAxis(ap=idx[:, 0:1], axis=0))\
                        .then_inc(gath[l], 16)

                def store(b):
                    wait_apart(pool, pool_steps, yo_rdy[l], b + 2)
                    pool.tensor_copy(idy[:, :], rowi[:, bass.ds(b, 1)]).then_inc(idy_rdy[l], 1)
                    wait_apart(pool, pool_steps, idy_rdy[l], b + 1)
                    pool.indirect_dma_start(out=ybuf, out_offset=bass.IndirectOffsetOnAxis(ap=idy[:, 0:1], axis=0),
                                            in_=yo[:, :], in_offset=None).then_inc(y_wr[l], 16)

                def next_gather(b):
                    pool.wait_ge(xg_used[l], b + 1)
                    pool.wait_ge(gath[l], (b + 1) * 16)
                    gather(b + 1)

                def split_ahead(b):
                    ord_next = table(pool, T_ORD + 1 + b, 0, NE - 1)
                    first_next = table(pool, T_FIRST + 1 + b, 0, 1)
                    with pool.If(first_next > 0):
                        rests(pool, nc.gpsimd, l, b + 1, ord_next, [3])

                def split_own(b):
                    ordn = table(pool, T_ORD + b, 0, NE - 1)
                    first = table(pool, T_FIRST + b, 0, 1)
                    with pool.If(first > 0):
                        rests(pool, nc.gpsimd, l, b, ordn, [5])

                gather(0)
                rests(pool, nc.gpsimd, l, 0, 0, [3])
                next_gather(0)
                rests(pool, nc.gpsimd, l, 0, 0, [5])
                next_gather(1)
                if l == 0:
                    pool.wait_ge(mod_used, 2)
                    for i in range(3):
                        pool.wait_ge(mblk_saved[i], 32)
                    load_mod(1, 0)
                split_ahead(0)
                with pool.Fori(1, n_blk) as b:
                    split_own(b)
                    next_gather(b + 1)
                    store(b - 1)
                    split_ahead(b)
                store(table(pool, T_LAST, 11, NB - 1))
                wait_apart(pool, pool_steps, gath[l], n_blk * 16 + 32)
                wait_apart(pool, pool_steps, y_wr[l], n_blk * 16)
                load_ln(l, 1)
                pool.dma_start(ypair[:, 0:2 * NT, :], ybuf[0:2 * NT * P, :].rearrange("(s p) d -> p s d", p=P))\
                    .then_inc(yg_ld[l], 16)
                if l == 0:
                    pool.wait_ge(x_rdy[0], NT)
            for t in range(NT):
                pool.wait_ge(x_rdy[1], t + 1)
                dst = y_prompt[0] if t == 0 else y_sample[0, (t - 1) * P:t * P, :]
                pool.dma_start(dst, x[:, t, :]).then_inc(out_done, 16)
            pool.wait_ge(out_done, 16 * (4 + NT))

        @block.scalar
        def _(act):
            small = 0

            def load(dst, src):
                nonlocal small
                act.dma_start(dst, src).then_inc(ld_small, 16)
                small += 16

            load(condr[:, 0, :], c_ctx.rearrange("(p k) -> p k", k=KD))
            load(condr[:, 1, :], c[0].rearrange("(p k) -> p k", k=KD))
            load(cst[:, :], consts)
            act.wait_ge(ld_small, small)
            act.activation(cond[:, :, :].rearrange("p k c -> p c k"), condr[:, :, :], ACT.Silu).then_inc(cond_rdy, 1)
            act.dma_start(badb[:, :], b_ada[0:1, :].to_broadcast([2, 6 * D])).then_inc(ld_bada, 16)
            load(x[:, 0, :], x_prompt[0])
            load(x[:, 1:3, :], x_sample[0].rearrange("(t p) d -> p t d", p=P))
            for l in range(LAYERS):
                load(wr[:, l, :, 0:NG], w_rg[l].rearrange("(p k) n -> p k n", k=KD))
                load(wr[:, l, :, NG:], w_re[l].rearrange("(p k) n -> p k n", k=KD))
                load(br[:, l, 0:NG], b_rg[l:l + 1, :].to_broadcast([P, NG]))
                load(br[:, l, NG:], b_re[l:l + 1, :].to_broadcast([P, NE]))
            load(lamb[:, :], lam_a.rearrange("a f d -> a (f d)").to_broadcast([P, 4 * HD]))
            load(subg[:, :], subln_a.to_broadcast([P, P]))
            act.wait_ge(lam_rdy, 1)
            act.activation(lam[:, 2:4], lam[:, 0:2], ACT.Exp).then_inc(lam_rdy, 1)

            def take_transposed(dst, done, ready):
                for t in range(NT):
                    act.wait_ge(done, t + 1)
                    act.activation(dst[:, :, t * P:(t + 1) * P], tile_ps(t).rearrange("p (k n) -> p k n", k=KD),
                                   ACT.Copy).then_inc(ready, 1)

            def take_ada(b):
                act.wait_ge(st_free, ada_end(b))
                if b >= 3:
                    act.wait_ge(mblk_saved[b % 3], 16 * (b // 3))
                act.activation(mst[:, b % 3, :], ps[0:2, ADA_BANK[b], :], ACT.Copy).then_inc(mblk_ev, 1)
                act.wait_ge(mblk_ev, b + 1)
                act.dma_start(mdram[1, :, b * 512:(b + 1) * 512], mst[:, b % 3, :]).then_inc(mblk_saved[b % 3], 16)

            for l in range(LAYERS):
                take_transposed(hT, hT_ps[l], hT_rdy[l])
                for g in range(3):
                    for t in range(NT):
                        if t < NT - 1:
                            act.wait_ge(qkv_done[l], 2 * g + t + 1)
                        else:
                            act.wait_ge(st_free, RING + QKV0[l] + 4 * (g + 1))
                        act.activation(qkv[:, t, g * D:(g + 1) * D], tile_ps(t), ACT.Copy).then_inc(qkv_ev[l], 1)
                for j in range(PAIRS):
                    act.wait_ge(qk_ps[l], 2 * j + 1)
                    act.activation(qT[:, j, :], ps[:, 4 + 2 * (j % 2), 0:NT * P], ACT.Copy).then_inc(qT_ev[l], 1)

                def exps(u):
                    t = u // PAIRS
                    n = keys[t]
                    e = prob[u % 2]
                    act.wait_ge(negm_rdy[l], u + 1)
                    if u >= 2:
                        act.wait_ge(pT_done[l], u - 1)
                    for h in range(2):
                        src = ps[:, 2 * (u % 2) + h, 0:n] if l == 0 else s_sb[:, h, 0:n]
                        ins = act.activation(e[:, h, 0:n], src, ACT.Exp, bias=negm[:, u % 2, h:h + 1],
                                             scale=SCALE if l == 0 else 1.0, accum_out=sums[:, u % 2, h:h + 1])
                    ins.then_inc(exp_done[l], 1)

                def take_pT(u):
                    n = keys[u // PAIRS]
                    act.wait_ge(pT_done[l], u + 1)
                    if u:
                        act.wait_ge(pv_done[l], u)
                    if l == 0:
                        act.activation(probT[:, 0, 0:n], ps[:, 4 + u % 2, 0:n], ACT.Copy).then_inc(pT_ev[l], 1)
                    else:
                        act.activation(probT[:, :, 0:n], ps[:, 4:6, 0:n], ACT.Copy).then_inc(pT_ev[l], 1)

                def take_o(u):
                    if l == 0 and u % PAIRS == PAIRS - 1:
                        act.wait_ge(pv_done[l], u + 1)
                        act.activation(o[:, u // PAIRS, :], tile_ps(3), ACT.Copy).then_inc(o_ev[l], 1)

                exps(0)
                exps(1)
                for u in range(UNITS):
                    take_pT(u)
                    if u + 2 < UNITS:
                        exps(u + 2)
                    take_o(u)
                take_transposed(oT, oT_ps[l], oT_rdy[l])
                if l == 0:
                    for b in range(4):
                        take_ada(b)
                take_transposed(hT, xT_ps[l], xT_rdy[l])
                if l == 0:
                    take_ada(4)
                rx = rt[:, 64:64 + 15]
                act.wait_ge(rt_dve[l], 1)
                act.activation(rx, rx, ACT.Exp).then_inc(rt_act[l], 1)

                act.wait_ge(tab_rdy[l], 1)
                n_blk = table(act, T_NBLK, 12, NB)

                def split_high(b, ordn, chunks):
                    for s in chunks:
                        act.wait_ge(moe_land[l][s], (ordn + 1) * 16)
                        if not (isinstance(b, int) and b == 0):
                            act.wait_ge(*chunk_use(l, s, b))
                        act.activation(wh[:, s, :], raw[:, s, :], ACT.Copy).then_inc(gu_high[l] if s < GU else dn_high[l], 1)

                def x_high(b):
                    act.wait_ge(xg_used[l], b + 1)
                    act.activation(xs[:, :, 0:BLK], ps[:, 0, :].rearrange("p (k n) -> p k n", k=KD), ACT.Copy)\
                        .then_inc(xsh_rdy[l], 1)

                def hidden(b):
                    act.wait_ge(gut_done[l], b * 2 + 1)
                    if not (isinstance(b, int) and b == 0):
                        act.wait_ge(hm_rdy[l], b)
                    act.activation(sg[:, :], ps[:, 3, 0:4 * BLK], ACT.Silu).then_inc(sg_rdy[l], 1)
                    act.wait_ge(hm_rdy[l], b + 1)
                    act.activation(hs[:, :, 0:BLK], hm[:, :].rearrange("p (k n) -> p k n", k=4), ACT.Copy)\
                        .then_inc(hh_rdy[l], 1)

                def body(b):
                    later = not isinstance(b, int)
                    act.wait_ge(*chunk_use(l, 1, b + 1))
                    if later:
                        act.wait_ge(gut_done[l], b * 2 - 1)
                    act.activation(gsb[:, :], ps[:, 1, :], ACT.Copy).then_inc(g_rdy[l], 1)
                    ord_next = table(act, T_ORD + 1 + b, 0, NE - 1)
                    first_next = table(act, T_FIRST + 1 + b, 0, 1)
                    with act.If(first_next > 0):
                        split_high(b + 1, ord_next, range(2))
                    if later:
                        ordn = table(act, T_ORD + b, 0, NE - 1)
                        first = table(act, T_FIRST + b, 0, 1)
                        with act.If(first > 0):
                            split_high(b, ordn, [4])
                    else:
                        split_high(b, 0, [4])
                    act.wait_ge(*chunk_use(l, 3, b + 1))
                    if later:
                        act.wait_ge(gut_done[l], b * 2)
                    act.activation(usb[:, :], ps[:, 2, :], ACT.Copy).then_inc(u_rdy[l], 1)
                    if later:
                        with act.If(first > 0):
                            split_high(b, ordn, [5])
                    else:
                        split_high(b, 0, [5])
                    x_high(b + 1)
                    hidden(b)
                    with act.If(first_next > 0):
                        split_high(b + 1, ord_next, range(2, GU))

                act.wait_ge(xmod_w[l], 16)
                act.wait_ge(rt_dve[l], 1)
                split_high(0, 0, range(GU))
                if l == 0:
                    take_ada(5)
                    for i in range(3):
                        act.wait_ge(mblk_saved[i], 32)
                x_high(0)
                body(0)
                with act.Fori(1, n_blk) as b:
                    body(b)
                if l == 0:
                    for b in range(6, 12):
                        take_ada(b)

        @block.tensor
        def _(pe):
            mm = nc.tensor.matmul
            pe.sem_inc(st_free, RING)
            pe.wait_ge(cond_rdy, 1)
            with pe.Fori(0, 4) as m:
                for s in range(RING):
                    pe.wait_ge(st_land[s], (m + 1) * 16)
                    if s % 2 == 0:
                        pe.wait_ge(ada_evac, m * 3 + s // 2 + 1)
                    for kk in range(4):
                        k = 4 * (s % 2) + kk
                        ins = mm(ps[0:2, s // 2, :], cond[:, k, :], raw[:, s, kk * 512:(kk + 1) * 512],
                                 start=(k == 0), stop=(k == KD - 1))
                    ins.then_inc(st_free, 1)

            def ada_block(b):
                out = ps[0:2, ADA_BANK[b], :]
                if b >= 2:
                    pe.wait_ge(mblk_ev, b - 1)
                for c in range(2):
                    n = ADA1[b // 6] + 2 * (b % 6) + c
                    wait_chunk(pe, n)
                    for kk in range(4):
                        k = 4 * c + kk
                        ins = mm(out, cond[:, k, :], raw[:, n % RING, kk * 512:(kk + 1) * 512],
                                 start=(k == 0), stop=False)
                    if c == 0:
                        ins.then_inc(st_free, 1)
                pe.wait_ge(mbias_ld, 16 * (b + 1))
                mm(out, cst[0:1, C_ONE:C_ONE + 2], mbias[:, :], start=False, stop=True).then_inc(st_free, 1)

            def transpose_tiles(src, ready, done):
                for t in range(NT):
                    pe.wait_ge(ready, t + 1)
                    for k in range(KD):
                        ins = nc.tensor.transpose(tile_ps(t)[:, k * P:(k + 1) * P],
                                                  src(t).rearrange("p (c k) -> p k c", k=KD)[:, k, :], ident)
                    ins.then_inc(done, 1)

            def project(lhs, nk, k0, slot, last, tile_done):
                for kk in range(nk):
                    k = k0 + kk
                    for t in range(NT):
                        for hf in range(2):
                            ins = mm(ps[:, 2 * t + hf, :], lhs[:, k, t * P:(t + 1) * P],
                                     raw[:, slot, kk * D + hf * 512:kk * D + (hf + 1) * 512],
                                     start=(k == 0), stop=(k == KD - 1))
                        if tile_done is not None and last and kk == nk - 1 and t < NT - 1:
                            ins.then_inc(tile_done, 1)
                ins.then_inc(st_free, 1)

            for l in range(LAYERS):
                transpose_tiles(lambda t: qkv[:, t, 0:D], h_rdy[l], hT_ps[l])
                pe.wait_ge(hT_rdy[l], NT)
                for g in range(3):
                    if g:
                        pe.wait_ge(qkv_ev[l], 3 * g)
                    for ck in range(4):
                        n = QKV0[l] + 4 * g + ck
                        wait_chunk(pe, n)
                        project(hT, 2, 2 * ck, n % RING, ck == 3, qkv_done[l])
                    if l == 1 and g < 2:
                        pe.wait_ge(hank_ld, 32 * (g + 1))
                        for i in range(6):
                            f = 6 * g + i
                            if f >= 2:
                                pe.wait_ge(flip_used, f - 1)
                            mm(ps[:, 6 + f % 2, :], cst[:, C_FLIP:C_FLIP + P], hank[:, i * 512:(i + 1) * 512],
                               start=True, stop=True).then_inc(flip_done, 1)
                if l == 0:
                    pe.wait_ge(roped, 4)
                else:
                    pe.wait_ge(flip_used, 12)
                pe.wait_ge(qkv_ev[l], 9)
                pe.wait_ge(ctx_ld[l], 32)
                for j in range(PAIRS):
                    bq, bk = 4 + 2 * (j % 2), 5 + 2 * (j % 2)
                    if j >= 2:
                        pe.wait_ge(qT_ev[l], j - 1)
                        pe.wait_ge(kT_ev[l], j - 1)
                    for t in range(NT):
                        ins = nc.tensor.transpose(ps[:, bq, t * P:(t + 1) * P], qkv[:, t, j * P:(j + 1) * P], ident)
                    ins.then_inc(qk_ps[l], 1)
                    kin = [qkv[:, 0, D + j * P:D + (j + 1) * P], kctx[:, j * P:(j + 1) * P],
                           qkv[:, 1, D + j * P:D + (j + 1) * P], qkv[:, 2, D + j * P:D + (j + 1) * P]]
                    for i in range(4):
                        ins = nc.tensor.transpose(ps[:, bk, i * P:(i + 1) * P], kin[i], ident)
                    ins.then_inc(qk_ps[l], 1)
                pe.wait_ge(qT_ev[l], PAIRS)
                pe.wait_ge(kT_ev[l], PAIRS)

                def values(t, i, lo, hi):
                    if t == 0:
                        return qkv[:, 0, 2 * D + lo:2 * D + hi]
                    return vctx[:, lo:hi] if i == 0 else qkv[:, i, 2 * D + lo:2 * D + hi]

                maps = 1 if l == 0 else 2

                def scores(u):
                    t, j = u // PAIRS, u % PAIRS
                    if u >= 2:
                        pe.wait_ge(exp_done[l] if l == 0 else negm_rdy[l], u - 1)
                    for h in range(2):
                        ins = mm(ps[:, 2 * (u % 2) + h, 0:keys[t]],
                                 qT[HD * h:HD * (h + 1), j, t * P:(t + 1) * P],
                                 kT[HD * h:HD * (h + 1), j, key0[t]:key0[t] + keys[t]], start=True, stop=True)
                    ins.then_inc(sc_done[l], 1)

                def transpose_prob(u):
                    nk = keys[u // PAIRS] // P
                    pe.wait_ge(comb_done[l] if l == 0 else exp_done[l], u + 1)
                    if u >= (2 if l == 0 else 1):
                        pe.wait_ge(pT_ev[l], u - 1 if l == 0 else u)
                    for h in range(maps):
                        for i in range(nk):
                            ins = nc.tensor.transpose(ps[:, 4 + (u % 2 if l == 0 else h), i * P:(i + 1) * P],
                                                      prob[u % 2][:, h, i * P:(i + 1) * P], ident)
                    ins.then_inc(pT_done[l], 1)

                def attend(u):
                    t, j = u // PAIRS, u % PAIRS
                    nk = keys[t] // P
                    pe.wait_ge(pT_ev[l], u + 1)
                    if j == 0 and t:
                        pe.wait_ge(o_ev[l], t)
                    w = P // maps
                    for h in range(maps):
                        lo = j * P + h * w
                        for i in range(nk):
                            ins = mm(tile_ps(3)[:, lo:lo + w], probT[:, h, i * P:(i + 1) * P], values(t, i, lo, lo + w),
                                     start=(i == 0), stop=(i == nk - 1))
                    ins.then_inc(pv_done[l], 1)

                scores(0)
                scores(1)
                for u in range(UNITS):
                    transpose_prob(u)
                    if u + 2 < UNITS:
                        scores(u + 2)
                    attend(u)

                transpose_tiles(lambda t: o[:, t, :], o_rdy[l], oT_ps[l])
                pe.wait_ge(oT_rdy[l], NT)
                k = 0
                for cidx, nk in enumerate(WO_K):
                    n = WO0[l] + cidx
                    wait_chunk(pe, n)
                    project(oT, nk, k, n % RING, False, None)
                    k += nk

                if l == 0:
                    for b in range(4):
                        ada_block(b)
                    pe.wait_ge(mblk_ev, 4)
                transpose_tiles(lambda t: qkv[:, t, 0:D], xm_rdy[l], xT_ps[l])
                pe.wait_ge(xT_rdy[l], NT)
                w36 = NG + NE
                for t in range(NT):
                    for k in range(KD):
                        ins = mm(ps[:, 6, t * w36:(t + 1) * w36], hT[:, k, t * P:(t + 1) * P], wr[:, l, k, :],
                                 start=(k == 0), stop=(k == KD - 1))
                ins.then_inc(rt_pe[l], 1)
                if l == 0:
                    ada_block(4)
                pe.wait_ge(rt_dve[l], 2)
                a_all = rt[:, 384:480].rearrange("p (t e) -> p t e", t=NT)
                for t in range(NT):
                    for i in range(t + 1):
                        mm(ps[:, 7, t * NE:(t + 1) * NE], tri if i == t else ones, a_all[:, i, :],
                           start=(i == 0), stop=(i == t))
                for t in range(NT):
                    ins = mm(ps[0:NE, 5, 0:1], a_all[:, t, :], ones[:, 0:1], start=(t == 0), stop=(t == NT - 1))
                ins.then_inc(rt_pe[l], 1)
                pe.wait_ge(rt_dve[l], 3)
                mm(ps[0:NE, 4, 0:2], tri[0:NE, 0:NE], rt[0:NE, 600:602], start=True, stop=True)
                mm(ps[:, 3, 0:NE], rt[0:NE, 640:768], tri[0:NE, 0:NE], start=True, stop=True).then_inc(rt_pe[l], 1)
                pe.wait_ge(rt_dve[l], 4)
                mm(ps[0:1, 2, T_LIST:T_LIST + NE], cst[0:NE, C_TOK:C_TOK + 1], rt[0:NE, 800:832], start=True, stop=True)
                mm(ps[0:1, 2, T_ORD:T_ORD + 48], rt[0:NE, 605:606], rt[0:NE, 832:880], start=True, stop=True)
                mm(ps[0:1, 2, T_FIRST:T_FIRST + 48], rt[0:NE, 601:602], rt[0:NE, 880:928], start=True, stop=True)
                mm(ps[0:1, 2, T_NACT:T_NACT + 1], rt[0:NE, 601:602], ones[0:NE, 0:1], start=True, stop=True)
                mm(ps[0:1, 2, T_NBLK:T_NBLK + 1], rt[0:NE, 600:601], ones[0:NE, 0:1], start=True, stop=True)\
                    .then_inc(rt_pe[l], 1)
                pe.wait_ge(rt_dve[l], 5)
                for i in range(2 * NT):
                    ins = mm(ps[0:BLK, 1, 0:NBX], rt[:, 1200 + i * BLK:1200 + (i + 1) * BLK],
                             rt[:, 1600 + i * NBX:1600 + (i + 1) * NBX], start=(i == 0), stop=(i == 2 * NT - 1))
                ins.then_inc(rt_pe[l], 1)

                pe.wait_ge(tab_rdy[l], 1)
                pe.wait_ge(tok_rdy[l], 1)
                n_blk = table(pe, T_NBLK, 12, NB)

                def transpose_x(b):
                    wait_apart(pe, pe_steps, gath[l], (b + 1) * 16)
                    for k in range(KD):
                        ins = nc.tensor.transpose(ps[:, 0, k * BLK:(k + 1) * BLK],
                                                  xg[:, :].rearrange("p (c k) -> p k c", k=KD)[:, k, :], ident64)
                    ins.then_inc(xg_used[l], 1)

                def gate_or_up(b, ordn, i):
                    for s in range(2 * i, 2 * i + 2):
                        pe.wait_ge(*high(l, s, ordn))
                        pe.wait_ge(*rest(l, s, ordn))
                        if s % 2 == 0 and not isinstance(b, int):
                            pe.wait_ge((g_rdy, u_rdy)[i][l], b)
                        for kk in range(4):
                            k = 4 * (s % 2) + kk
                            for part in (wh, wl):
                                ins = mm(ps[:, 1 + i, :], xs[:, k, :], part[:, s, kk * 512:(kk + 1) * 512],
                                         start=(k == 0 and part is wh), stop=(k == KD - 1 and part is wl))
                        ins.then_inc(gu_used[l], 1)

                def down(b, ordn):
                    pe.wait_ge(hh_rdy[l], b + 1)
                    pe.wait_ge(hl_rdy[l], b + 1)
                    pe.wait_ge(yo_rdy[l], b + 1)
                    for s in range(GU, RING):
                        pe.wait_ge(*high(l, s, ordn))
                        pe.wait_ge(*rest(l, s, ordn))
                        for jj in range(2):
                            j = 2 * (s - GU) + jj
                            for hf in range(2):
                                for part in (wh, wl):
                                    ins = mm(ps[:, 5 + hf, :], hs[:, j, :],
                                             part[:, s, jj * D + hf * 512:jj * D + (hf + 1) * 512],
                                             start=(j == 0 and part is wh), stop=(j == 3 and part is wl))
                        ins.then_inc(dn_used[l], 1)

                def body(b):
                    later = not isinstance(b, int)
                    ordn = table(pe, T_ORD + b, 0, NE - 1) if later else 0
                    pe.wait_ge(xsh_rdy[l], b + 1)
                    pe.wait_ge(xsl_rdy[l], b + 1)
                    gate_or_up(b, ordn, 0)
                    if later:
                        down(b - 1, table(pe, T_ORD - 1 + b, 0, NE - 1))
                    gate_or_up(b, ordn, 1)
                    for i, (src, ready) in enumerate(((gsb, g_rdy), (usb, u_rdy))):
                        pe.wait_ge(ready[l], b + 1)
                        if later:
                            pe.wait_ge((sg_rdy, hm_rdy)[i][l], b)
                        for j in range(4):
                            ins = mm(ps[:, 3 + i, j * BLK:(j + 1) * BLK],
                                     src[:, :].rearrange("p (c j) -> p j c", j=4)[:, j, :], stack2, start=True, stop=True)
                        ins.then_inc(gut_done[l], 1)
                        if i == 0:
                            transpose_x(b + 1)

                if l == 0:
                    ada_block(5)
                    pe.wait_ge(mblk_ev, 5)
                transpose_x(0)
                body(0)
                with pe.Fori(1, n_blk) as b:
                    body(b)
                last_blk = table(pe, T_LAST, 11, NB - 1)
                down(last_blk, table(pe, T_ORD + last_blk, 0, NE - 1))
                if l == 0:
                    for b in range(6, 12):
                        ada_block(b)
                    pe.wait_ge(mblk_ev, 12)

        @block.vector
        def _(dve):
            v = nc.vector

            def chain(ins):
                dve.drain()
                return ins

            dve.sem_inc(ada_evac, 3)
            for l in range(LAYERS):
                dve.sem_inc(yo_rdy[l], 1)
                dve.sem_inc(gu_rest[l], 3)
                for s in (up_rest, dn_rest, dn2_rest):
                    dve.sem_inc(s[l], 1)
            dve.wait_ge(ld_bada, 16)
            with dve.Fori(0, 4) as m:
                for i in range(3):
                    dve.wait_ge(st_free, m * RING + RING + 2 * i + 2)
                    at = bass.ds(m * 1536 + i * 512, 512)
                    v.tensor_tensor(mrow[:, at], ps[0:2, i, :], badb[:, at], ALU.add).then_inc(ada_evac, 1)

            dve.wait_ge(ld_small, 16 * (3 + 2 + 4 * LAYERS + 2))
            lv = lamb[:, :].rearrange("p (a b d) -> p a b d", a=2, b=2)
            chain(v.tensor_tensor(lv[:, :, 0, :], lv[:, :, 0, :], lv[:, :, 1, :], ALU.mult))
            v.tensor_reduce(lam[:, 0:2], lv[:, :, 0, :], AX, ALU.add).then_inc(lam_rdy, 1)
            chain(v.tensor_scalar(subg[:, :], subg[:, :], 1.0 - LAM_INIT, None, ALU.mult))
            dve.wait_ge(lam_rdy, 2)
            chain(v.tensor_tensor(lam[:, 0:1], lam[:, 2:3], lam[:, 3:4], ALU.subtract))
            chain(v.tensor_scalar(lam[:, 0:1], lam[:, 0:1], LAM_INIT, None, ALU.add))

            def modulate(l, stage, ready):
                dve.wait_ge(mod_ld, 64 * (2 * l + stage + 1))
                for t in range(NT):
                    sc = 0 if t == 0 else 2
                    chain(v.scalar_tensor_tensor(qkv[:, t, 0:D], modb[:, sc, :], 1.0, x[:, t, :], ALU.add, ALU.mult))
                    v.tensor_tensor(qkv[:, t, 0:D], qkv[:, t, 0:D], modb[:, sc + 1, :], ALU.add).then_inc(ready, 1)
                dve.drain()
                dve.sem_inc(mod_used, 1)

            def guess(r, a):
                ri = r.bitcast(I32)
                chain(v.tensor_single_scalar(ri, a.bitcast(I32), 1, op=ALU.arith_shift_right))
                chain(v.tensor_scalar(ri, ri, -1.0, float(0x5F3759DF), ALU.mult, ALU.add))

            def newton(r, a, tmp):
                chain(v.tensor_tensor(tmp, r, r, ALU.mult))
                chain(v.scalar_tensor_tensor(tmp, tmp, -0.5, a, ALU.mult, ALU.mult))
                chain(v.scalar_tensor_tensor(r, tmp, 1.5, r, ALU.add, ALU.mult))

            def rsqrt(r, a, tmp):
                guess(r, a)
                for _ in range(3):
                    newton(r, a, tmp)

            def fold(l, stage):
                dve.wait_ge(lnb_ld, 64 * (2 * l + stage + 1))
                dve.wait_ge(mod_ld, 64 * (2 * l + stage + 2))
                for sc in (0, 2):
                    chain(v.scalar_tensor_tensor(t1[:, :], modb[:, sc, :], 1.0, lnb[:, 3, :], ALU.add, ALU.mult))
                    v.tensor_tensor(modb[:, sc + 1, :], t1[:, :], modb[:, sc + 1, :], ALU.add)
                    chain(v.scalar_tensor_tensor(modb[:, sc, :], modb[:, sc, :], 1.0, lnb[:, 2, :], ALU.add, ALU.mult))

            def layer_norm(l, stage, src, ready):
                dve.wait_ge(lnb_ld, 64 * (2 * l + stage + 1))
                for t in range(NT):
                    chain(v.tensor_tensor(t1[:, :], src(t), lnb[:, 0 if t == 0 else 1, :], ALU.mult))
                    chain(v.scalar_tensor_tensor(x[:, t, :], x[:, t, :], ALPHA, t1[:, :], ALU.mult, ALU.add))
                    for i in range(2):
                        v.bn_stats(st[:, i, :], x[:, t, i * 512:(i + 1) * 512])
                    dve.drain()
                    chain(v.bn_aggr(mv[:, t, :], st[:, :, :].rearrange("p a b -> p (a b)")))
                chain(v.tensor_scalar(var[:, 0:NT], mv[:, :, 1], EPS, None, ALU.add))
                rsqrt(rstd[:, 0:NT], var[:, 0:NT], newt[:, 0:NT])
                for t in range(NT):
                    chain(v.tensor_scalar(x[:, t, :], x[:, t, :], mv[:, t, 0:1], rstd[:, t:t + 1], ALU.subtract, ALU.mult))
                    if ready is not None:
                        sc = 0 if t == 0 else 2
                        chain(v.tensor_tensor(qkv[:, t, 0:D], x[:, t, :], modb[:, sc, :], ALU.mult))
                        v.tensor_tensor(qkv[:, t, 0:D], qkv[:, t, 0:D], modb[:, sc + 1, :], ALU.add).then_inc(ready, 1)
                if ready is not None:
                    dve.drain()
                    dve.sem_inc(mod_used, 1)
                for t in range(NT):
                    chain(v.tensor_tensor(x[:, t, :], x[:, t, :], lnb[:, 2, :], ALU.mult))
                    chain(v.tensor_tensor(x[:, t, :], x[:, t, :], lnb[:, 3, :], ALU.add))
                    if stage == 1:
                        dve.sem_inc(x_rdy[l], 1)

            for l in range(LAYERS):
                if l == 0:
                    dve.wait_ge(mrow_saved, 16)
                if l == 0:
                    modulate(l, 0, h_rdy[l])
                    for g in range(2):
                        dve.wait_ge(qkv_ev[l], 3 * (g + 1))
                        for t in range(1, NT):
                            hv = qkv[:, t, g * D:(g + 1) * D].rearrange("p (h a b j) -> p h a b j", a=2, b=2, j=16)\
                                .rearrange("p h a b j -> p (h a) b j")
                            tb = C_ROPE + (t - 1) * 64
                            cosb = cst[:, tb:tb + 32].unsqueeze(1).to_broadcast([P, HEADS, 32])\
                                .rearrange("p h (a j) -> p h a j", a=2)
                            sinb = cst[:, tb + 32:tb + 64].unsqueeze(1).to_broadcast([P, HEADS, 32])\
                                .rearrange("p h (a j) -> p h a j", a=2)
                            x1, x2 = (hv[:, :, b, :].rearrange("p (h a) j -> p h a j", a=2) for b in range(2))
                            tmp = [rope[:, i, :].rearrange("p (h a j) -> p h a j", h=HEADS, a=2) for i in range(4)]
                            v.tensor_tensor(tmp[0], x1, cosb, ALU.mult)
                            v.tensor_tensor(tmp[1], x2, sinb, ALU.mult)
                            v.tensor_tensor(tmp[2], x2, cosb, ALU.mult)
                            chain(v.tensor_tensor(tmp[3], x1, sinb, ALU.mult))
                            v.tensor_tensor(x1, tmp[0], tmp[1], ALU.subtract)
                            v.tensor_tensor(x2, tmp[2], tmp[3], ALU.add).then_inc(roped, 1)
                            dve.drain()
                else:
                    for i in range(3):
                        dve.wait_ge(mblk_saved[i], 64)
                    for f in range(12):
                        dve.wait_ge(flip_done, f + 1)
                        v.tensor_tensor(btab[:, f * 512:(f + 1) * 512].rearrange("p (a n) -> p a n", n=GRID_W),
                                        ps[:, 6 + f % 2, :].rearrange("p (a n) -> p a n", n=GRID_W),
                                        cst[:, C_WIN:C_WIN + GRID_W].unsqueeze(1).to_broadcast([P, 8, GRID_W]),
                                        ALU.add).then_inc(flip_used, 1)
                for j in range(PAIRS):
                    dve.wait_ge(qk_ps[l], 2 * j + 2)
                    v.tensor_copy(kT[:, j, :], ps[:, 5 + 2 * (j % 2), :]).then_inc(kT_ev[l], 1)

                def maxima(u):
                    t, j = u // PAIRS, u % PAIRS
                    n = keys[t]
                    sc = ps[:, 2 * (u % 2):2 * (u % 2) + 2, :]
                    dve.wait_ge(sc_done[l], u + 1)
                    if l == 0:
                        chain(v.tensor_reduce(sums[:, u % 2, :], sc[:, :, 0:n], AX, ALU.max))
                        v.tensor_scalar(negm[:, u % 2, :], sums[:, u % 2, :], -SCALE, None, ALU.mult)\
                            .then_inc(negm_rdy[l], 1)
                        return
                    if u:
                        dve.wait_ge(exp_done[l], u)
                    v.tensor_scalar(s_sb[:, :, 0:P], sc[:, :, 0:P], SCALE, None, ALU.mult)
                    if t:
                        m0 = 2 - 2 * (t - 1)
                        bias = btab[:, :].rearrange("p (h n) -> p h n", h=HEADS)[:, 2 * j:2 * j + 2,
                                                                                m0 * GRID_W:(m0 + ROWS) * GRID_W]
                        v.scalar_tensor_tensor(s_sb[:, :, P:n], sc[:, :, P:n], SCALE, bias, ALU.mult, ALU.add)
                    dve.drain()
                    chain(v.tensor_reduce(negm[:, u % 2, :], s_sb[:, :, 0:n], AX, ALU.max))
                    v.tensor_scalar(negm[:, u % 2, :], negm[:, u % 2, :], -1.0, None, ALU.mult).then_inc(negm_rdy[l], 1)

                def combine(u):
                    t, j = u // PAIRS, u % PAIRS
                    n = keys[t]
                    e = prob[u % 2]
                    dve.wait_ge(exp_done[l], u + 1)
                    if l == 1:
                        at = (t % 2) * HEADS + 2 * j
                        v.reciprocal(rsum[:, at:at + 2], sums[:, u % 2, :])
                        dve.drain()
                        return
                    chain(v.reciprocal(rsum[:, 0:2], sums[:, u % 2, :]))
                    chain(v.tensor_tensor(rsum[:, 1:2], rsum[:, 1:2], lam[:, 0:1], ALU.mult))
                    chain(v.tensor_scalar(e[:, 1, 0:n], e[:, 1, 0:n], rsum[:, 1:2], None, ALU.mult))
                    v.scalar_tensor_tensor(e[:, 0, 0:n], e[:, 0, 0:n], rsum[:, 0:1], e[:, 1, 0:n],
                                           ALU.mult, ALU.subtract).then_inc(comb_done[l], 1)
                    dve.drain()

                def take_o(t):
                    dve.wait_ge(pv_done[l], PAIRS * (t + 1))
                    v.tensor_tensor(o[:, t, :].rearrange("p (h d) -> p h d", h=HEADS),
                                    tile_ps(3).rearrange("p (h d) -> p h d", h=HEADS),
                                    rsum[:, (t % 2) * HEADS:(t % 2 + 1) * HEADS].unsqueeze(2).to_broadcast([P, HEADS, HD]), ALU.mult)
                    dve.drain()
                    dve.sem_inc(o_ev[l], 1)
                    dve.sem_inc(o_rdy[l], 1)

                def head_norm(t, step):
                    ov = o[:, t, :].rearrange("p (h d) -> p h d", d=P)
                    if step == 0:
                        dve.wait_ge(o_ev[l], t + 1)
                        chain(v.tensor_tensor(t1[:, :], o[:, t, :], o[:, t, :], ALU.mult))
                    elif step == 1:
                        chain(v.tensor_reduce(var[:, :], t1[:, :].rearrange("p (h d) -> p h d", d=P), AX, ALU.add))
                        chain(v.tensor_scalar(var[:, :], var[:, :], 1.0 / P, EPS, ALU.mult, ALU.add))
                    elif step == 2:
                        guess(rstd[:, :], var[:, :])
                        newton(rstd[:, :], var[:, :], newt[:, :])
                    elif step < 5:
                        newton(rstd[:, :], var[:, :], newt[:, :])
                    elif step == 5:
                        chain(v.tensor_tensor(ov, ov, rstd[:, :].unsqueeze(2).to_broadcast([P, 8, P]), ALU.mult))
                    else:
                        v.tensor_tensor(ov, ov, subg[:, :].unsqueeze(1).to_broadcast([P, 8, P]), ALU.mult)\
                            .then_inc(o_rdy[l], 1)
                        dve.drain()

                if l == 1:
                    dve.drain()
                maxima(0)
                maxima(1)
                combine(0)
                for u in range(UNITS):
                    if u + 1 < UNITS:
                        combine(u + 1)
                    if u + 2 < UNITS:
                        maxima(u + 2)
                    if l == 1 and u % PAIRS == PAIRS - 1:
                        take_o(u // PAIRS)
                    if l == 0 and u >= PAIRS and u % PAIRS < 7:
                        head_norm(u // PAIRS - 1, u % PAIRS)
                if l == 0:
                    for step in range(7):
                        head_norm(NT - 1, step)
                fold(l, 0)
                dve.wait_ge(st_free, RING + WO0[l] + RING)
                layer_norm(l, 0, tile_ps, xm_rdy[l])

                def col(a, n):
                    return rt[:, a:a + n]

                lg = col(128, NT * 36).rearrange("p (t n) -> p t n", t=NT)
                gl, el = lg[:, :, 0:NG], lg[:, :, NG:]
                rx = col(64, 15).rearrange("p (t n) -> p t n", t=NT)
                iota = cst[:, C_IOTA:C_IOTA + P]

                def b3(a, n):
                    return a.unsqueeze(2).to_broadcast([P, NT, n])

                def iota3(n):
                    return iota[:, 0:n].unsqueeze(1).to_broadcast([P, NT, n])

                def first_max(vals, n, mx, one):
                    tmp = col(288, NT * n).rearrange("p (t n) -> p t n", t=NT)
                    chain(v.tensor_reduce(mx, vals, AX, ALU.max))
                    chain(v.tensor_tensor(tmp, vals, b3(mx, n), ALU.is_equal))
                    chain(v.tensor_scalar(tmp, tmp, -1000.0, 1000.0, ALU.mult, ALU.add))
                    chain(v.tensor_tensor(tmp, tmp, iota3(n), ALU.add))
                    chain(v.tensor_reduce(col(20, NT), tmp, AX, ALU.min))
                    chain(v.tensor_tensor(one, iota3(n), b3(col(20, NT), n), ALU.is_equal))

                a_all = col(384, 96).rearrange("p (t e) -> p t e", t=NT)
                e1 = col(480, 96).rearrange("p (t e) -> p t e", t=NT)
                e2 = col(1024, 96).rearrange("p (t e) -> p t e", t=NT)
                dve.wait_ge(rt_pe[l], 1)
                chain(v.tensor_tensor(lg, ps[:, 6, 0:NT * 36].rearrange("p (t n) -> p t n", t=NT),
                                      br[:, l, :].unsqueeze(1).to_broadcast([P, NT, 36]), ALU.add))
                oneg = col(32, NT * NG).rearrange("p (t n) -> p t n", t=NT)
                first_max(gl, NG, col(0, NT), oneg)
                v.tensor_tensor(rx[:, :, 0:NG], gl, b3(col(0, NT), NG), ALU.subtract)
                pen = col(48, NT * NG).rearrange("p (t n) -> p t n", t=NT)
                chain(v.tensor_scalar(pen, oneg, BIG, -BIG, ALU.mult, ALU.add))
                e4 = el.rearrange("p t (g n) -> p t g n", g=NG)
                for t in range(NT):
                    chain(v.tensor_tensor(e4[:, t], e4[:, t], oneg[:, t, :].unsqueeze(2).to_broadcast([P, NG, EPG]), ALU.mult))
                    chain(v.tensor_tensor(e4[:, t], e4[:, t], pen[:, t, :].unsqueeze(2).to_broadcast([P, NG, EPG]), ALU.add))
                first_max(el, NE, col(3, NT), e1)
                chain(v.scalar_tensor_tensor(el, e1, -2 * BIG, el, ALU.mult, ALU.add))
                first_max(el, NE, col(6, NT), e2)
                v.tensor_tensor(rx[:, :, NG], col(6, NT), col(3, NT), ALU.subtract).then_inc(rt_dve[l], 1)
                v.tensor_tensor(a_all, e1, e2, ALU.add).then_inc(rt_dve[l], 1)
                dve.wait_ge(rt_pe[l], 2)
                cnt = rt[0:NE, 590:591]
                chain(v.tensor_copy(cnt, ps[0:NE, 5, 0:1]))
                chain(v.tensor_scalar(rt[0:NE, 592:598], cst[0:NE, C_THR:C_THR + 6], cnt, None, ALU.is_lt))
                chain(v.tensor_reduce(rt[0:NE, 600:601], rt[0:NE, 592:598], AX, ALU.add))
                v.tensor_copy(rt[0:NE, 601:602], rt[0:NE, 592:593])
                v.tensor_scalar(rt[0:NE, 640:768], cst[0:NE, C_ONE:C_ONE + P], rt[0:NE, 600:601], None, ALU.mult)
                dve.drain()
                dve.sem_inc(rt_dve[l], 1)
                dve.wait_ge(rt_pe[l], 3)
                first_b, ordn, last_b = rt[0:NE, 604:605], rt[0:NE, 605:606], rt[0:NE, 606:607]
                chain(v.tensor_copy(rt[0:NE, 604:606], ps[0:NE, 4, 0:2]))
                v.tensor_tensor(last_b, first_b, rt[0:NE, 600:601], ALU.add)
                used = rt[0:NE, 601:602]
                v.tensor_scalar(rt[0:NE, 800:832], iota[0:NE, 0:NE], ordn, used, ALU.is_equal, ALU.mult)
                v.tensor_scalar(rt[0:NE, 880:928], iota[0:NE, 0:48], first_b, used, ALU.is_equal, ALU.mult)
                chain(v.tensor_scalar(rt[0:NE, 832:880], iota[0:NE, 0:48], first_b, None, ALU.is_ge))
                v.scalar_tensor_tensor(rt[0:NE, 832:880], iota[0:NE, 0:48], last_b, rt[0:NE, 832:880],
                                       ALU.is_lt, ALU.mult)
                dve.drain()
                dve.sem_inc(rt_dve[l], 1)
                sp_ = col(928, 96).rearrange("p (t e) -> p t e", t=NT)
                chain(v.tensor_copy(sp_, ps[:, 7, 0:96].rearrange("p (t e) -> p t e", t=NT)))
                chain(v.tensor_scalar(col(768, NE), ps[:, 3, 0:NE], float(BLK), None, ALU.mult))
                chain(v.tensor_tensor(sp_, sp_, col(768, NE).unsqueeze(1).to_broadcast([P, NT, NE]), ALU.add))
                for k, one in enumerate((e1, e2)):
                    chain(v.tensor_tensor(one, one, sp_, ALU.mult))
                    chain(v.tensor_reduce(col(1184, 2 * NT).rearrange("p (t k) -> p t k", k=2)[:, :, k], one, AX, ALU.add))
                chain(v.tensor_copy(sloti[:, :], col(1184, 2 * NT)))
                si = rt[:, 2000:2000 + 12].bitcast(I32)
                v.tensor_single_scalar(si[:, 0:6], sloti[:, :], 6, op=ALU.arith_shift_right)
                chain(v.tensor_single_scalar(si[:, 6:12], sloti[:, :], BLK - 1, op=ALU.bitwise_and))
                sf = col(2016, 12)
                chain(v.tensor_copy(sf, si))
                rowf = col(2032, 2 * NT)
                for k in range(TOPK):
                    v.tensor_scalar(rowf.rearrange("p (t k) -> p t k", k=TOPK)[:, :, k], cst[:, C_TOK:C_TOK + NT],
                                    1.0 + k * NT * P, None, ALU.add)
                dve.drain()
                for i in range(2 * NT):
                    v.tensor_scalar(col(1200 + i * BLK, BLK), iota[:, 0:BLK], sf[:, 6 + i:7 + i], None, ALU.is_equal)
                    v.tensor_scalar(col(1600 + i * NBX, NBX), iota[:, 0:NBX], sf[:, i:i + 1],
                                    rowf[:, i:i + 1], ALU.is_equal, ALU.mult)
                dve.drain()
                dve.sem_inc(rt_dve[l], 1)
                dve.wait_ge(rt_pe[l], 4)
                chain(v.tensor_scalar(tabi[:, T_LAST:T_N], ps[0:1, 2, T_NBLK:T_NBLK + 1], -1.0, None, ALU.add))
                v.tensor_copy(tabi[:, 0:T_LAST], ps[0:1, 2, 0:T_LAST]).then_inc(tab_rdy[l], 1)
                dve.wait_ge(rt_pe[l], 5)
                val, empty, half = (rt[0:BLK, 2048 + i * NBX:2048 + (i + 1) * NBX] for i in range(3))
                chain(v.tensor_scalar(val, ps[0:BLK, 1, 0:NBX], -1.0, None, ALU.add))
                chain(v.tensor_scalar(empty, val, 0.0, None, ALU.is_lt))
                chain(v.tensor_scalar(half, cst[0:BLK, C_TOK:C_TOK + 1].to_broadcast([BLK, NBX]),
                                      float(TOPK * NT * P + 1), None, ALU.add))
                chain(v.tensor_tensor(half, half, empty, ALU.mult))
                chain(v.tensor_tensor(rowi[:, :], val, half, ALU.add))
                chain(v.tensor_scalar(half, val, float(NT * P), float(NT * P), ALU.is_ge, ALU.mult))
                chain(v.tensor_tensor(val, val, half, ALU.subtract))
                v.tensor_scalar(toki[:, :], val, 0.0, None, ALU.max).then_inc(tok_rdy[l], 1)
                dve.wait_ge(rt_act[l], 1)
                chain(v.tensor_reduce(col(9, NT), rx[:, :, 0:NG], AX, ALU.add))
                chain(v.tensor_scalar(col(12, NT), rx[:, :, NG], 1.0, None, ALU.add))
                chain(v.tensor_tensor(col(9, NT), col(9, NT), col(12, NT), ALU.mult))
                chain(v.reciprocal(gatew[:, 0, :], col(9, NT)))
                chain(v.tensor_tensor(gatew[:, 1, :], gatew[:, 0, :], rx[:, :, NG], ALU.mult))

                dve.wait_ge(tab_rdy[l], 1)
                last_blk = table(dve, T_LAST, 11, NB - 1)

                def split_rest(b, ordn, chunks):
                    rests(dve, v, l, b, ordn, [s for s in chunks if s not in POOL_CHUNKS])

                def x_rest(b):
                    dve.wait_ge(xsh_rdy[l], b + 1)
                    v.tensor_tensor(xs[:, :, BLK:2 * BLK], ps[:, 0, :].rearrange("p (k n) -> p k n", k=KD),
                                    xs[:, :, 0:BLK].bitcast(F32), ALU.subtract).then_inc(xsl_rdy[l], 1)

                def y_sum(b):
                    dve.wait_ge(*chunk_use(l, RING - 1, b + 1))
                    chain(v.tensor_copy(yl[:, :], ps_t[BLK:P, 5 * 512:7 * 512]))
                    if not (isinstance(b, int) and b == 0):
                        dve.wait_ge(y_wr[l], b * 16)
                    v.tensor_tensor(yo[:, :], ps_t[0:BLK, 5 * 512:7 * 512], yl[:, :], ALU.add).then_inc(yo_rdy[l], 1)

                def hidden(b):
                    dve.wait_ge(sg_rdy[l], b + 1)
                    dve.wait_ge(gut_done[l], b * 2 + 2)
                    if not (isinstance(b, int) and b == 0):
                        dve.wait_ge(hh_rdy[l], b)
                        dve.wait_ge(hl_rdy[l], b)
                    v.tensor_tensor(hm[:, :], sg[:, :], ps[:, 4, 0:4 * BLK], ALU.mult).then_inc(hm_rdy[l], 1)
                    dve.wait_ge(hh_rdy[l], b + 1)
                    v.tensor_tensor(hs[:, :, BLK:2 * BLK], hm[:, :].rearrange("p (k n) -> p k n", k=4),
                                    hs[:, :, 0:BLK].bitcast(F32), ALU.subtract).then_inc(hl_rdy[l], 1)

                def body(b, before=None):
                    ord_next = table(dve, T_ORD + 1 + b, 0, NE - 1)
                    first_next = table(dve, T_FIRST + 1 + b, 0, 1)
                    with dve.If(first_next > 0):
                        split_rest(b + 1, ord_next, range(2))
                    if before is not None:
                        ordn = table(dve, T_ORD + b, 0, NE - 1)
                        first = table(dve, T_FIRST + b, 0, 1)
                        with dve.If(first > 0):
                            split_rest(b, ordn, range(GU, RING))
                    else:
                        split_rest(b, 0, range(GU, RING))
                    x_rest(b + 1)
                    hidden(b)
                    if before is not None:
                        y_sum(before)
                    with dve.If(first_next > 0):
                        split_rest(b + 1, ord_next, range(2, GU))

                split_rest(0, 0, range(GU))
                x_rest(0)
                body(0)
                body(1, 0)
                with dve.Fori(1, last_blk) as b:
                    body(b + 1, b)
                y_sum(last_blk)
                if l == 0:
                    fold(l, 1)
                dve.wait_ge(yg_ld[l], 16)
                for t in range(NT):
                    chain(v.tensor_scalar(o[:, t, :], ypair[:, t, :], gatew[:, 0, t:t + 1], None, ALU.mult))
                    chain(v.scalar_tensor_tensor(o[:, t, :], ypair[:, NT + t, :], gatew[:, 1, t:t + 1], o[:, t, :],
                                                 ALU.mult, ALU.add))
                layer_norm(l, 1, lambda t: o[:, t, :], h_rdy[1] if l == 0 else None)


_INS = ['x_prompt', 'x_sample', 'cache_a_k', 'cache_a_v', 'cache_b_k', 'cache_b_v', 'c', 'c_ctx', 'w_ada', 'b_ada',
        'ln_g', 'ln_b', 'w_qkv_a', 'lam_a', 'subln_a', 'w_o_a', 'w_qkv_b', 'rpb_b', 'w_o_b', 'w_rg', 'b_rg', 'w_re',
        'b_re', 'w_gate', 'w_up', 'w_down']
_OUTS = [(1, 128, 1024), (1, 256, 1024), (1, 1, 128, 16, 64), (1, 1, 128, 8, 128), (1, 1, 128, 16, 64),
         (1, 1, 128, 16, 64)]


def kernel(**inputs):
    import numpy as _np
    import concourse.bacc as _bacc
    from concourse import mybir as _mybir
    from concourse.bass_utils import run_bass_kernel_spmd as _run

    nc = _bacc.Bacc("TRN2", target_bir_lowering=False, num_devices=1)
    arrays, args = {}, []
    for name in _INS:
        a = _np.ascontiguousarray(inputs[name])
        arrays[f"in_{name}_dram"] = a
        args.append(nc.dram_tensor(f"in_{name}_dram", a.shape, _mybir.dt.from_np(a.dtype), kind="ExternalInput").ap())
    a = constants()
    arrays["in_consts_dram"] = a
    args.append(nc.dram_tensor("in_consts_dram", a.shape, _mybir.dt.from_np(a.dtype), kind="ExternalInput").ap())
    for i, shape in enumerate(_OUTS):
        args.append(nc.dram_tensor(f"out_{i}_dram", shape, _mybir.dt.float32, kind="ExternalOutput").ap())
    backbone_kernel(nc, *args)
    r = _run(nc, [arrays], core_ids=[0])
    return tuple(r.results[0][f"out_{i}_dram"] for i in range(len(_OUTS)))
```
